# Optimizing a Trainium2 kernel written in Bass

```python
import math
import jax, jax.numpy as jnp
from jax import lax
import numpy as np

D_MODEL = 1024
BATCH = 1
SEQ = 512
DEPTH = 1
DEC_BATCH = 8
DEC_SEQ = 8
PAST_LEN = 4096
PAGE_SIZE = 128

N_MEM = 256
CONV_CH = 512
CONV_K = 31
DN_HEADS = 4
DN_DK = 128
DN_DV = 128
DN_QK = DN_HEADS * DN_DK
DN_V = DN_HEADS * DN_DV
QKV_W = 2 * DN_QK + DN_V
SHORT_K = 4
CHUNK = 64
X_HEADS = 4
X_HEAD_DIM = D_MODEL // X_HEADS
D_FF = 4 * D_MODEL
DEEPNORM_ALPHA = (2 * DEPTH) ** 0.25
DEEPNORM_BETA = (8 * DEPTH) ** -0.25
LN_EPS = 1e-5
RMS_EPS = 1e-6
L2_EPS = 1e-6
IN_SIZES = (2 * CONV_CH, QKV_W, DN_V, DN_HEADS, DN_HEADS, D_MODEL, D_MODEL)
IN_OFFSETS = tuple(sum(IN_SIZES[:i + 1]) for i in range(len(IN_SIZES) - 1))
N_IN = sum(IN_SIZES)

kernel_name = 'hybrid_conformer_gdn_decode_step'

def layer_norm(x, g, b):
    xf = x.astype(jnp.float32)
    mu = xf.mean(-1, keepdims=True)
    var = jnp.square(xf - mu).mean(-1, keepdims=True)
    return ((xf - mu) * lax.rsqrt(var + LN_EPS) * g.astype(jnp.float32) + b.astype(jnp.float32)).astype(x.dtype)

def l2_norm(x):
    xf = x.astype(jnp.float32)
    return xf * lax.rsqrt(jnp.sum(xf * xf, -1, keepdims=True) + L2_EPS)

def causal_dwconv(hist, x, w):
    xx = jnp.concatenate([hist.astype(x.dtype), x], axis=1)
    y = lax.conv_general_dilated(xx, w.astype(x.dtype)[:, None, :], (1,), 'VALID',
                                 dimension_numbers=('NWC', 'WIO', 'NWC'),
                                 feature_group_count=x.shape[-1])
    return y, xx[:, xx.shape[1] - (w.shape[0] - 1):]

def to_chunks(t, B, n, C, pad):
    t = t.astype(jnp.float32)
    t = jnp.pad(t, [(0, 0), (0, pad)] + [(0, 0)] * (t.ndim - 2))
    t = t.reshape((B, n, C) + t.shape[2:])
    t = jnp.swapaxes(t, 2, 3)
    return jnp.moveaxis(t, 1, 0)

def gated_delta_rule(q, k, v, beta, logdecay, s0):
    B, L, H, DK = q.shape
    C = min(CHUNK, L)
    n = -(-L // C)
    pad = n * C - L
    qc, kc, vc = (to_chunks(t, B, n, C, pad) for t in (q, k, v))
    bc, gc = (to_chunks(t, B, n, C, pad) for t in (beta, logdecay))
    G = jnp.cumsum(gc, axis=-1)
    idx = jnp.arange(C)
    tril = idx[:, None] >= idx[None, :]
    strict = idx[:, None] > idx[None, :]
    diff = G[..., :, None] - G[..., None, :]
    decay_mat = jnp.where(tril, jnp.exp(jnp.where(tril, diff, 0.0)), 0.0)
    kk = jnp.einsum('nbhid,nbhjd->nbhij', kc, kc)
    A = jnp.where(strict, bc[..., :, None] * kk * decay_mat, 0.0)
    M = A + jnp.eye(C, dtype=jnp.float32)
    eG = jnp.exp(G)
    rhs = jnp.concatenate([(bc * eG)[..., None] * kc, bc[..., None] * vc], axis=-1)
    sol = lax.linalg.triangular_solve(M, rhs, left_side=True, lower=True, unit_diagonal=True)
    Wc, Uv = sol[..., :DK], sol[..., DK:]
    Aqk = jnp.einsum('nbhid,nbhjd->nbhij', qc, kc) * decay_mat
    eGC = jnp.exp(G[..., -1])
    k_tail = kc * jnp.exp(G[..., -1:] - G)[..., None]

    def step(S, xs):
        w_, uv_, q_, aqk_, eg_, egc_, kt_ = xs
        U = uv_ - jnp.einsum('bhck,bhkv->bhcv', w_, S)
        o = eg_[..., None] * jnp.einsum('bhck,bhkv->bhcv', q_, S) + jnp.einsum('bhij,bhjv->bhiv', aqk_, U)
        S = egc_[..., None, None] * S + jnp.einsum('bhck,bhcv->bhkv', kt_, U)
        return S, o

    s_fin, o = lax.scan(step, s0.astype(jnp.float32), (Wc, Uv, qc, Aqk, eG, eGC, k_tail))
    o = jnp.swapaxes(jnp.moveaxis(o, 0, 1), 2, 3).reshape(B, n * C, H, -1)[:, :L]
    return o, s_fin

def hybrid_layer(x, mem_k, mem_v, conv_hist, qkv_hist, s0, p):
    B, L, _ = x.shape
    proj = x @ p['w_in']
    glu, qkv, og, beta_raw, dec_raw, g_a, g_b = jnp.split(proj, IN_OFFSETS, axis=-1)
    glu = glu + p['b_glu']
    u = glu[..., :CONV_CH] * jax.nn.sigmoid(glu[..., CONV_CH:])
    cv, conv_new = causal_dwconv(conv_hist, u, p['w_dw'])
    cv = jax.nn.silu(layer_norm(cv + p['b_dw'], p['ln_conv_g'], p['ln_conv_b']))
    br_a = cv @ p['w_conv_out']
    qkv, qkv_new = causal_dwconv(qkv_hist, qkv, p['w_short'])
    qkv = jax.nn.silu(qkv)
    q, k, v = jnp.split(qkv, (DN_QK, 2 * DN_QK), axis=-1)
    q = l2_norm(q.reshape(B, L, DN_HEADS, DN_DK)) * (DN_DK ** -0.5)
    k = l2_norm(k.reshape(B, L, DN_HEADS, DN_DK))
    v = v.reshape(B, L, DN_HEADS, DN_DV)
    beta = jax.nn.sigmoid(beta_raw.astype(jnp.float32))
    logdecay = -jnp.exp(p['a_log'].astype(jnp.float32)) * jax.nn.softplus(
        dec_raw.astype(jnp.float32) + p['dt_bias'].astype(jnp.float32))
    o, s_new = gated_delta_rule(q, k, v, beta, logdecay, s0)
    o = o * lax.rsqrt(jnp.mean(o * o, -1, keepdims=True) + RMS_EPS) * p['dn_norm_g'].astype(jnp.float32)
    o = o * jax.nn.silu(og.reshape(B, L, DN_HEADS, DN_DV).astype(jnp.float32))
    br_b = o.reshape(B, L, DN_V).astype(x.dtype) @ p['w_dn_out']
    mixed = jax.nn.sigmoid(g_a) * br_a + jax.nn.sigmoid(g_b) * br_b
    h = layer_norm(DEEPNORM_ALPHA * x + mixed @ p['w_o'], p['ln1_g'], p['ln1_b'])
    xq = (h @ p['w_xq']).reshape(B, L, X_HEADS, X_HEAD_DIM)
    sc = jnp.einsum('blhd,bmhd->bhlm', xq, mem_k.astype(xq.dtype)).astype(jnp.float32) * (X_HEAD_DIM ** -0.5)
    pr = jax.nn.softmax(sc, axis=-1).astype(h.dtype)
    xo = jnp.einsum('bhlm,bmhd->blhd', pr, mem_v.astype(h.dtype)).reshape(B, L, D_MODEL) @ p['w_xo']
    h = layer_norm(DEEPNORM_ALPHA * h + xo, p['ln2_g'], p['ln2_b'])
    ff = jnp.square(jax.nn.relu(h @ p['w_ff1'])) @ p['w_ff2']
    y = layer_norm(DEEPNORM_ALPHA * h + ff, p['ln3_g'], p['ln3_b'])
    return y, conv_new, qkv_new, s_new

def setup_inputs(seed: int = 0) -> dict:
    key = jax.random.key(seed)
    ks = iter(jax.random.split(key, 48))

    def nrm(shape, scale):
        return jax.random.normal(next(ks), shape, jnp.float32) * scale

    def gain(n):
        return 1.0 + nrm((DEPTH, n), 0.05)

    dt = jnp.exp(jax.random.uniform(next(ks), (DEPTH, DN_HEADS), jnp.float32,
                                    minval=math.log(1e-3), maxval=math.log(1e-1)))
    w_mem_kv = jnp.concatenate([nrm((DEPTH, D_MODEL, D_MODEL), D_MODEL ** -0.5),
                                nrm((DEPTH, D_MODEL, D_MODEL), D_MODEL ** -0.5 * DEEPNORM_BETA)], axis=-1)
    return {
        'x_prompt': nrm((BATCH, SEQ, D_MODEL), 1.0),
        'x_sample': nrm((DEC_BATCH, DEC_SEQ, D_MODEL), 1.0),
        'mem_prompt': nrm((BATCH, N_MEM, D_MODEL), 1.0),
        'state_conv': nrm((DEPTH, DEC_BATCH, CONV_K - 1, CONV_CH), 0.5),
        'state_qkv_conv': nrm((DEPTH, DEC_BATCH, SHORT_K - 1, QKV_W), 1.0),
        'state_delta': nrm((DEPTH, DEC_BATCH, DN_HEADS, DN_DK, DN_DV), DN_DK ** -0.5),
        'cache_mem_k': nrm((DEPTH, DEC_BATCH, N_MEM, X_HEADS, X_HEAD_DIM), 1.0),
        'cache_mem_v': nrm((DEPTH, DEC_BATCH, N_MEM, X_HEADS, X_HEAD_DIM), DEEPNORM_BETA),
        'w_in': nrm((DEPTH, D_MODEL, N_IN), D_MODEL ** -0.5),
        'b_glu': nrm((DEPTH, 2 * CONV_CH), 0.02),
        'w_dw': nrm((DEPTH, CONV_K, CONV_CH), CONV_K ** -0.5),
        'b_dw': nrm((DEPTH, CONV_CH), 0.02),
        'ln_conv_g': gain(CONV_CH),
        'ln_conv_b': nrm((DEPTH, CONV_CH), 0.02),
        'w_conv_out': nrm((DEPTH, CONV_CH, D_MODEL), CONV_CH ** -0.5 * DEEPNORM_BETA),
        'w_short': nrm((DEPTH, SHORT_K, QKV_W), SHORT_K ** -0.5),
        'a_log': jnp.log(jax.random.uniform(next(ks), (DEPTH, DN_HEADS), jnp.float32, minval=1.0, maxval=16.0)),
        'dt_bias': dt + jnp.log(-jnp.expm1(-dt)),
        'dn_norm_g': gain(DN_DV),
        'w_dn_out': nrm((DEPTH, DN_V, D_MODEL), DN_V ** -0.5 * DEEPNORM_BETA),
        'w_o': nrm((DEPTH, D_MODEL, D_MODEL), D_MODEL ** -0.5 * DEEPNORM_BETA),
        'ln1_g': gain(D_MODEL),
        'ln1_b': nrm((DEPTH, D_MODEL), 0.02),
        'w_xq': nrm((DEPTH, D_MODEL, D_MODEL), D_MODEL ** -0.5),
        'w_mem_kv': w_mem_kv,
        'w_xo': nrm((DEPTH, D_MODEL, D_MODEL), D_MODEL ** -0.5 * DEEPNORM_BETA),
        'ln2_g': gain(D_MODEL),
        'ln2_b': nrm((DEPTH, D_MODEL), 0.02),
        'w_ff1': nrm((DEPTH, D_MODEL, D_FF), D_MODEL ** -0.5 * DEEPNORM_BETA),
        'w_ff2': nrm((DEPTH, D_FF, D_MODEL), D_FF ** -0.5 * DEEPNORM_BETA),
        'ln3_g': gain(D_MODEL),
        'ln3_b': nrm((DEPTH, D_MODEL), 0.02),
    }

def reference(x_prompt, x_sample, mem_prompt, state_conv, state_qkv_conv, state_delta, cache_mem_k, cache_mem_v,
              w_in, b_glu, w_dw, b_dw, ln_conv_g, ln_conv_b, w_conv_out, w_short, a_log, dt_bias, dn_norm_g,
              w_dn_out, w_o, ln1_g, ln1_b, w_xq, w_mem_kv, w_xo, ln2_g, ln2_b, w_ff1, w_ff2, ln3_g, ln3_b):
    B = x_prompt.shape[0]
    h_p, h_s = x_prompt, x_sample
    p_conv, p_qkv, p_delta, p_mk, p_mv = [], [], [], [], []
    s_conv, s_qkv, s_delta = [], [], []
    for l in range(DEPTH):
        p = dict(w_in=w_in[l], b_glu=b_glu[l], w_dw=w_dw[l], b_dw=b_dw[l], ln_conv_g=ln_conv_g[l],
                 ln_conv_b=ln_conv_b[l], w_conv_out=w_conv_out[l], w_short=w_short[l], a_log=a_log[l],
                 dt_bias=dt_bias[l], dn_norm_g=dn_norm_g[l], w_dn_out=w_dn_out[l], w_o=w_o[l],
                 ln1_g=ln1_g[l], ln1_b=ln1_b[l], w_xq=w_xq[l], w_xo=w_xo[l], ln2_g=ln2_g[l], ln2_b=ln2_b[l],
                 w_ff1=w_ff1[l], w_ff2=w_ff2[l], ln3_g=ln3_g[l], ln3_b=ln3_b[l])
        mk, mv = jnp.split(mem_prompt @ w_mem_kv[l], 2, axis=-1)
        mk = mk.reshape(B, N_MEM, X_HEADS, X_HEAD_DIM)
        mv = mv.reshape(B, N_MEM, X_HEADS, X_HEAD_DIM)
        h_p, c_new, q_new, d_new = hybrid_layer(
            h_p, mk, mv,
            jnp.zeros((B, CONV_K - 1, CONV_CH), x_prompt.dtype),
            jnp.zeros((B, SHORT_K - 1, QKV_W), x_prompt.dtype),
            jnp.zeros((B, DN_HEADS, DN_DK, DN_DV), jnp.float32), p)
        p_conv.append(c_new)
        p_qkv.append(q_new)
        p_delta.append(d_new.astype(x_prompt.dtype))
        p_mk.append(mk)
        p_mv.append(mv)
        h_s, c2, q2, d2 = hybrid_layer(h_s, cache_mem_k[l], cache_mem_v[l], state_conv[l],
                                       state_qkv_conv[l], state_delta[l], p)
        s_conv.append(c2.astype(state_conv.dtype))
        s_qkv.append(q2.astype(state_qkv_conv.dtype))
        s_delta.append(d2.astype(state_delta.dtype))
    return (h_p, h_s, jnp.stack(p_conv), jnp.stack(p_qkv), jnp.stack(p_delta), jnp.stack(p_mk), jnp.stack(p_mv),
            jnp.stack(s_conv), jnp.stack(s_qkv), jnp.stack(s_delta))


_drawn_inputs = setup_inputs


def setup_inputs(seed=0):
    import zlib

    import numpy as np

    out = dict(_drawn_inputs(seed))
    spreads = {}
    factors = {'b_dw': 8.0,
     'ln_conv_g': 8.0,
     'ln_conv_b': 36.781,
     'dn_norm_g': 8.0,
     'ln1_b': 2.828,
     'ln2_b': 2.725,
     'ln3_b': 2.745}
    for name, (base, spread) in spreads.items():
        noise = np.random.default_rng([zlib.crc32(name.encode()), seed]).standard_normal(out[name].shape)
        drawn = base * np.exp(spread * noise) if base else spread * noise
        out[name] = __import__('jax').numpy.asarray(drawn.astype(out[name].dtype))
    for name, factor in factors.items():
        out[name] = (out[name] * factor).astype(out[name].dtype)
    return out
```

```python
import numpy as np

import concourse.bass as bass
from concourse import mybir
from concourse.alu_op_type import AluOpType as ALU

D_MODEL, SEQ, DEC_BATCH, DEC_SEQ, N_MEM = 1024, 512, 8, 8, 256
CONV_CH, CONV_K, SHORT_K = 512, 31, 4
HEADS, DK = 4, 128
X_HEADS, X_DIM = 4, 256
D_FF = 4 * D_MODEL
ALPHA = 2.0 ** 0.25
LN_EPS, RMS_EPS, L2_EPS = 1e-5, 1e-6, 1e-6

P = 128
SAMPLE = DEC_BATCH * DEC_SEQ
TOK = SEQ + SAMPLE
HALF = TOK // 2
KB = D_MODEL // P
RING = 4
CT = CONV_CH // P
QT = 3 * HEADS
TILES = SEQ // P
CH, QH = CONV_K - 1, SHORT_K - 1
UP, US = CH + SEQ, CH + DEC_SEQ
RP, RS = QH + SEQ, QH + DEC_SEQ
QUARTERS = D_FF // D_MODEL

C_QKV, C_GLU, C_OG, C_MIX, C_WO, C_MEM, C_XQ, C_XO, C_FF = 0, 12, 20, 24, 48, 56, 72, 80, 88
CHUNKS = 152
O_QKV, O_GLU, O_OG, O_GATE, O_WO, O_MEM, O_XQ, O_XO, O_FF = 0, 12, 20, 24, 40, 48, 64, 72, 80

WIDTHS = [("b_glu", 8), ("b_dw", 4), ("cg", 4), ("cb", 4), ("dng", 1), ("g1", 8), ("b1", 8), ("g2", 8), ("b2", 8),
          ("g3", 8), ("b3", 8), ("w_dw", CT * CONV_K), ("w_short", QT * SHORT_K), ("a_log", 4), ("dt_bias", 4)]
PAR = {n: sum(w for _, w in WIDTHS[:i]) for i, (n, _) in enumerate(WIDTHS)}
NPAR = sum(w for _, w in WIDTHS)
LEVELS = [1, 2, 4, 8, 16, 32, 64]


def build(nc, A):
    f32, f32r = mybir.dt.float32, mybir.dt.float32r
    ACT = mybir.ActivationFunctionType
    X = mybir.AxisListType.X
    mul, add, sub = ALU.mult, ALU.add, ALU.subtract

    BASE, KIB = 16512, 1024
    R0, R1, R2, R3 = 48, 84, 120, 156

    def at(name, kib, shape, dtype=f32):
        return nc.alloc_sbuf_tensor_at(name, shape, dtype, offset=BASE + int(kib * KIB))

    def pair(name, kib, n=KB, w=TOK):
        return (at(name + "_hi", kib, [P, n, w], f32r), at(name + "_lo", kib + n * w * 4 / KIB, [P, n, w], f32r))

    raw = at("w_raw", 0, [P, RING, KB, P])
    whi = at("w_hi", 16, [P, RING, KB, P], f32r)
    wlo = at("w_lo", 32, [P, RING, KB, P], f32r)

    x = pair("x", R0)
    kv = at("kv", R0, [P, 4, 2 * X_HEADS * N_MEM])
    h2 = pair("h2", R0)

    xraw = at("xraw", R1, [P, KB, TOK])
    qraw = at("qraw", R1, [P, QT, RP + DEC_BATCH * RS])
    sst = at("sst", R1, [P, HEADS, DEC_BATCH, DK])
    pst = at("pst", R1 + 34, [P, HEADS, DK])
    z = pair("z", R1)
    memraw = at("memraw", R1, [P, KB, N_MEM])
    mem = pair("mem", R1 + 8, KB, N_MEM)
    ao = pair("ao", R1)

    u = at("u", R2, [P, CT, UP + DEC_BATCH * US])
    qhist = at("qhist", R2 + 14, [P, QT, DEC_BATCH * QH])
    qlast = at("qlast", R2 + 15.25, [P, QT, (1 + DEC_BATCH) * QH])
    wbd = at("wbd", R2 + 16.75, [P, KB, 8])
    sig = at("sig", R2 + 16.75, [P, 2, TOK])
    bdw = pair("bdw", R2 + 21.5, KB, 8)
    tmp = at("tmp", R2 + 21.5, [P, 2, TOK])
    nrm = at("nrm", R2 + 26, [P, 2, TOK])
    dl = at("dl", R2, [P, 2, 8, SEQ])
    sw = at("sw", R2, [P, 8, HEADS, SAMPLE])
    skt = at("skt", R2 + 8, [P, HEADS, DK])
    sz = at("sz", R2 + 10, [P, HEADS, DK])
    su = at("su", R2 + 12, [P, HEADS, DK])
    sktm = at("sktm", R2 + 14, [P, 2, DEC_BATCH, DK])
    szt = at("szt", R2 + 22, [P, HEADS, SAMPLE])
    sld = at("sld", R2 + 24, [P, HEADS, DK])
    lmask = at("lmask", R2 + 32, [P, len(LEVELS), P])
    mixed = pair("mixed", R2)
    h1 = pair("h1", R2)
    hid = pair("hid", R2)

    qkv = at("qkv", R3, [P, QT, TOK])
    ga = at("ga", R3, [P, 2, TOK])
    gb = at("gb", R3 + 4.5, [P, 2, TOK])
    mx = at("mx", R3 + 9, [P, 2, 2, TOK])
    res = at("res", R3, [P, KB, TOK])
    aq = at("aq", R3, [P, KB, TOK])
    mk = at("mk", R3 + 18, [P, KB, N_MEM])
    mv = at("mv", R3 + 26, [P, 2, D_MODEL])
    ht = at("ht", R3 + 18, [P, 2, TOK])
    hs = at("hs", R3 + 22.5, [P, 2, TOK])
    sgate = at("sgate", R3 + 27, [P, HEADS, TOK])
    cv = at("cv", R3 + 36, [P, CT, TOK])
    lns = at("lns", R3 + 34, [P, 2, TOK])
    lnt = at("lnt", R3 + 38.5, [P, 2, TOK])
    ap = at("att_p", R3 + 34, [P, 4, N_MEM])
    apt = at("att_pt", R3 + 38, [P, 2, SEQ])
    ssc = at("att_s", R3 + 42, [P, 2, 2 * P])
    cst = at("cst", R3 + 45, [P, 328])
    ident, triu, triu8, same8 = cst[:, 0:128], cst[:, 128:256], cst[:, 256:320], cst[:, 320:328]
    ones = at("ones", R3 + 46.5, [P, 4, P])
    par = at("par", R3 + 48.5, [P, NPAR])
    sm = at("sm", R3 + 49.75, [P, 260])
    eps_ln, eps_l2 = sm[:, 256:257], sm[:, 257:258]
    assert RMS_EPS == L2_EPS

    def cols(a, n, c):
        return sm[:, a:a + n * c].rearrange("p (t c) -> p t c", c=c)

    bd, beta, ld, gcol, sp0, sp1 = cols(0, 5, 8), cols(40, 5, 4), cols(60, 5, 4), cols(80, 5, 4), cols(100, 5, 4), \
        cols(120, 5, 4)
    nega, etail, eglast, seglast, stail = sm[:, 140:144], cols(144, 2, 4), cols(152, 2, 4), cols(160, 4, 8), \
        sm[:, 192:196]
    amax, asum = sm[:, 200:204], sm[:, 208:212]
    ltp = sm[:, 216:220]

    ps = [nc.alloc_psum_tensor(f"bank{i}", [P, 512], f32) for i in range(8)]
    HALVES = (slice(0, HALF), slice(HALF, TOK))
    PT, ST, SL = slice(0, SEQ), slice(SEQ, TOK), slice(0, SAMPLE)

    def out_pair(o):
        return ps[2 * (o % 2)], ps[2 * (o % 2) + 1]

    def pc(name, i=0):
        return par[:, PAR[name] + i:PAR[name] + i + 1]

    def bc(a, n):
        return a.unsqueeze(2).broadcast_to([a.shape[0], a.shape[1], n])

    def rep(a, n):
        return a.unsqueeze(1).broadcast_to([a.shape[0], n, a.shape[1]])

    def tiled(a, n=P):
        return a.rearrange("p (c i) -> p c i", i=n)

    def u_s(j):
        return u[:, j, UP:].rearrange("p (b t) -> p b t", t=US)

    K_, V_, NB_, QK_, X_, Y_, P_, W_ = range(8)
    S_NB, S_QK, S_X, S_Y, S_P, S_W, S_D, S_E = range(8)

    def dt(hh, k):
        return tiled(dl[:, hh, k])

    sems = {}

    def S(name):
        if name not in sems:
            sems[name] = nc.alloc_semaphore(name)
        return sems[name]

    raw_loaded = [S(f"raw_loaded{i}") for i in range(RING)]
    hi_ready, lo_ready, gemm_done = S("hi_ready"), S("lo_ready"), S("gemm_done")
    taken = [S("taken0"), S("taken1")]
    stored = S("stored")
    N_STORES = 1 + 2 * CT + 1 + 1 + 2 + KB
    CONSTS = 7

    def at_head(pr, hh):
        return 2 * pr + hh + 1

    def at_level(pr, n, hh):
        return (pr * len(LEVELS) + n) * 2 + hh + 1

    def at_tile(pr, c, hh):
        return (pr * TILES + c) * 2 + hh + 1

    def ln(name, what, steps, n):
        return S("ln_" + what), (int(name[2]) - 1) * steps + n

    class Chain:

        def __init__(self, eng, name, start=0):
            self.eng, self.sem, self.n, self.start = eng, S(name), 0, start

        def step(self, ins):
            self.n += 1
            ins.then_inc(self.sem, 1)

        def wait(self, back=0):
            if self.n > back:
                self.eng.wait_ge(self.sem, self.start + self.n - back)

        def __call__(self, ins):
            self.step(ins)
            self.wait()

    block_ctx = nc.Block()
    block = block_ctx.__enter__()

    @block.sync
    def _(sp):
        sp.dma_start(xraw[:, 0:4], A["xT"][:, 0:4]).then_inc(S("x_loaded0"), 16)
        sp.dma_start(xraw[:, 4:8], A["xT"][:, 4:8]).then_inc(S("x_loaded1"), 16)
        for s in range(RING):
            sp.dma_start(raw[:, s], A["w"][s]).then_inc(raw_loaded[s], 16)
            if s == 0:
                sp.dma_start(wbd[:], A["wbd"][:]).then_inc(S("par_loaded"), 16)
                sp.dma_start(par[:], A["par"][:]).then_inc(S("par_loaded"), 16)
                sp.dma_start(qhist[:], A["qhist"][:]).then_inc(S("par_loaded"), 16)
        sp.dma_start(cst[:], A["cst"][:]).then_inc(S("cst_loaded"), 16)
        sp.dma_start(lmask[:], A["lmask"][:]).then_inc(S("cst_loaded"), 16)
        for j in range(CT):
            sp.dma_start(u_s(j)[:, :, 0:CH], A["chist"][:, j]).then_inc(S("cst_loaded"), 16)

        def weights(first, last):
            with sp.Fori(0, (last - first) // RING) as g:
                for s in range(RING):
                    chunk = sp.snap(g * RING + first + s)
                    used = sp.snap(g * RING + first + s - RING + 1)
                    sp.wait_ge(lo_ready, used)
                    sp.dma_start(raw[:, s], A["w"][chunk]).then_inc(raw_loaded[s], 16)

        weights(4, C_OG)
        sp.wait_ge(S("qraw_free"), 1)
        sp.dma_start(sst[:], A["sdelta"][:]).then_inc(S("sst_loaded"), 16)
        weights(C_OG, C_WO + 4)
        sp.wait_ge(gemm_done, C_WO)
        sp.dma_start(memraw[:], A["memT"][:]).then_inc(S("mem_loaded"), 16)
        weights(C_WO + 4, C_XQ + 4)
        sp.wait_ge(*ln("ln1", "res", KB, KB))
        for i in range(2 * DEC_BATCH):
            if i >= 4:
                sp.wait_ge(S("kv_used"), i - 3)
            sp.dma_start(kv[:, i % 4], (A["kT"] if i < DEC_BATCH else A["v"])[i % DEC_BATCH])\
              .then_inc(S(f"kv_loaded{i % 4}"), 16)
            if i == 3:
                weights(C_XQ + 4, C_XO + 4)
        weights(C_XO + 4, CHUNKS)
        sp.wait_ge(stored, 16 * N_STORES)

    @block.gpsimd
    def _(pool):
        for i, v in enumerate((1.0, 1 / 128, 1 / 512, 1 / 1024)):
            nc.gpsimd.memset(ones[:, i], v).then_inc(S("consts"), 1)
        nc.gpsimd.memset(eps_ln, LN_EPS).then_inc(S("consts"), 1)
        nc.gpsimd.memset(eps_l2, L2_EPS).then_inc(S("consts"), 1)
        nc.gpsimd.memset(u[:, :, 0:CH], 0.0).then_inc(S("consts"), 1)
        with pool.Fori(0, CHUNKS // RING) as g:
            for s in range(RING):
                pool.wait_ge(hi_ready, g * RING + s + 1)
                nc.gpsimd.tensor_tensor(wlo[:, s], raw[:, s], whi[:, s].bitcast(f32), sub).then_inc(lo_ready, 1)

    @block.tensor
    def _(pe):
        SPANS = ((0, HALF), (HALF, TOK))
        every = [(kb, None) for kb in range(KB)]

        def gemm(slot, out, xs, kbs, spans=SPANS):
            for i, (kb, ready) in enumerate(kbs):
                if ready is not None:
                    pe.wait_ge(*ready)
                for bank, (a, b) in zip(out, spans):
                    for j, (w, m) in enumerate(((whi, xs[0]), (whi, xs[1]), (wlo, xs[0]))):
                        ins = nc.tensor.matmul(bank[:, 0:b - a], lhsT=w[:, slot, kb], rhs=m[:, kb, a:b],
                                               start=(i == 0 and j == 0), stop=(i == len(kbs) - 1 and j == 2))
            return ins

        def phase(c0, o0, n, xs, kbs, spans=SPANS):
            def group(g, fresh=False):
                for s in range(RING):
                    pe.wait_ge(lo_ready, g * RING + c0 + s + 1)
                    if not (fresh and s < 2):
                        pe.wait_ge(taken[s % 2], g * 2 + (o0 + s) // 2)
                    gemm(s, out_pair(o0 + s), xs, kbs, spans).then_inc(gemm_done, 1)
            if n == RING:
                return group(0)
            if o0 == 0:
                group(0, True)
            with pe.Fori(1 if o0 == 0 else 0, n // RING) as g:
                group(g)

        def ln_average(name):
            pe.wait_ge(*ln(name, "sum", 2 * KB, 2 * KB))
            for i in range(2):
                for h, half in enumerate(HALVES):
                    ins = nc.tensor.matmul(ps[4 + 2 * i + h][:, 0:HALF], lhsT=ones[:, 3], rhs=lns[:, i, half],
                                           start=True, stop=True)
            ins.then_inc(S("ln_avg"), 1)

        pe.wait_ge(S("bdw_split"), 2)
        pe.wait_ge(S("x_lo"), KB)
        for t in range(5):
            n = P if t < TILES else SAMPLE
            for kb in range(KB):
                for j, (a, w) in enumerate(((x[0], bdw[0]), (x[1], bdw[0]), (x[0], bdw[1]))):
                    ins = nc.tensor.matmul(ps[4][0:n, 8 * t:8 * t + 8], lhsT=a[:, kb, t * P:t * P + n],
                                           rhs=w[:, kb], start=(kb == 0 and j == 0), stop=(kb == KB - 1 and j == 2))
        ins.then_inc(S("bd_done"), 1)

        phase(C_QKV, O_QKV, 12, x, every)
        phase(C_GLU, O_GLU, 8, x, every)

        pe.wait_ge(S("ld_ready"), 1)
        pe.wait_ge(S("cst_loaded"), 16 * (2 + CT))
        nc.tensor.matmul(ps[4][:, 64:64 + 16], lhsT=triu, rhs=ld[:, 0:TILES], start=True, stop=True)
        nc.tensor.matmul(ps[4][SL, 80:84], lhsT=triu8[SL], rhs=ld[SL, TILES], start=True, stop=True)\
            .then_inc(S("g_done"), 1)
        pe.wait_ge(S("consts"), CONSTS)
        pe.wait_ge(S("gcol_ready"), 1)
        for i in range(2 * HEADS):
            pe.wait_ge(S("l2_sq"), i + 1)
            if i >= 2:
                pe.wait_ge(S("l2_root"), 2 * (i - 1))
            for h, half in enumerate(HALVES):
                ins = nc.tensor.matmul(ps[4 + 2 * (i % 2) + h][:, 0:HALF], lhsT=ones[:, 0], rhs=sig[:, i % 2, half],
                                       start=True, stop=True)
            ins.then_inc(S("l2_sum"), 1)

        phase(C_OG, O_OG, 4, x, every)

        T = nc.tensor
        pe.wait_ge(S("sld_ready"), 1)
        for h in range(HEADS):
            ins = T.matmul(ps[4][:, h * SAMPLE:(h + 1) * SAMPLE], lhsT=sld[SL, h], rhs=triu8[SL], start=True, stop=True)
        ins.then_inc(S("s_grow"), 1)
        for h in range(HEADS):
            k, q = qkv[:, HEADS + h, ST], qkv[:, h, ST]
            T.matmul(ps[5][SL, h * SAMPLE:(h + 1) * SAMPLE], lhsT=k, rhs=k, start=True, stop=True)
            ins = T.matmul(ps[5][SL, (4 + h) * SAMPLE:(5 + h) * SAMPLE], lhsT=k, rhs=q, start=True, stop=True)
        ins.then_inc(S("s_kk"), 1)
        for h in range(HEADS):
            ins = T.transpose(ps[6][SL, h * DK:(h + 1) * DK], qkv[:, HEADS + h, ST], ident)
        ins.then_inc(S("s_kt"), 1)

        def sw_all(bank, a, b, width=SAMPLE, off=0):
            for h in range(HEADS):
                ins = T.matmul(bank[SL, off + h * width:off + (h + 1) * width], lhsT=a(h), rhs=b(h), start=True,
                               stop=True)
            return ins

        for n in range(3):
            pe.wait_ge(S("s_as"), n + 1)
            if n > 0:
                pe.wait_ge(S("s_xy"), 2 * n)
            sw_all(ps[4], lambda h: sw[SL, S_W, h], lambda h: sw[SL, S_X, h] if n else ident[SL, SL])\
                .then_inc(S("s_ax"), 1)
            if n > 0:
                pe.wait_ge(S("s_p"), n)
                sw_all(ps[5], lambda h: sw[SL, S_Y, h], lambda h: sw[SL, S_P, h])
                sw_all(ps[5], lambda h: sw[SL, S_P, h], lambda h: sw[SL, S_Y, h], off=256).then_inc(S("s_xax"), 1)
        pe.wait_ge(S("sst_loaded"), 16)
        pe.wait_ge(S("s_scaled"), 2)
        for h in range(HEADS):
            for b in range(DEC_BATCH):
                ins = T.matmul(ps[6][:, h * SAMPLE + 8 * b:h * SAMPLE + 8 * b + 8], lhsT=sst[:, h, b],
                               rhs=qkv[:, HEADS + h, SEQ + 8 * b:SEQ + 8 * b + 8], start=True, stop=True)
        ins.then_inc(S("s_ks"), 1)
        pe.wait_ge(S("s_zt"), 1)
        for h in range(HEADS):
            ins = T.transpose(ps[7][SL, h * DK:(h + 1) * DK], szt[:, h], ident)
        ins.then_inc(S("s_ztt"), 1)
        pe.wait_ge(S("s_z"), 1)
        pe.wait_ge(S("s_xy"), 6)
        sw_all(ps[4], lambda h: sw[SL, S_Y, h], lambda h: sz[SL, h], width=DK).then_inc(S("s_yz"), 1)
        pe.wait_ge(S("s_u"), 1)
        for h in range(HEADS):
            T.matmul(ps[5][:, h * SAMPLE:(h + 1) * SAMPLE], lhsT=su[SL, h], rhs=sw[SL, S_QK, h], start=True, stop=False,
                     skip_group_check=True)
            for b in range(DEC_BATCH):
                ins = T.matmul(ps[5][:, h * SAMPLE + 8 * b:h * SAMPLE + 8 * b + 8], lhsT=sst[:, h, b],
                               rhs=qkv[:, h, SEQ + 8 * b:SEQ + 8 * b + 8], start=False, stop=(b == DEC_BATCH - 1),
                               skip_group_check=True)
        ins.then_inc(S("s_o"), 1)
        for h in range(HEADS):
            pe.wait_ge(S("s_ktm"), h + 1)
            if h > 0:
                pe.wait_ge(S("s_new"), 3 * h)
            else:
                pe.wait_ge(S("s_z"), 1)
            for b in range(DEC_BATCH):
                ins = T.matmul(ps[6 + b // 4][:, (b % 4) * DK:(b % 4 + 1) * DK], lhsT=sktm[SL, h % 2, b],
                               rhs=su[SL, h], start=True, stop=True)
            ins.then_inc(S("s_ds"), 1)

        pe.wait_ge(S("s_new"), 3 * HEADS)
        pe.wait_ge(S("s_otaken"), 1)
        for pr in range(2):
            HH = range(2)
            q = [tiled(qkv[:, 2 * pr + hh, PT]) for hh in HH]
            k = [tiled(qkv[:, HEADS + 2 * pr + hh, PT]) for hh in HH]
            v = [tiled(qkv[:, 2 * HEADS + 2 * pr + hh, PT]) for hh in HH]
            b0, b1 = (ps[4], ps[6]), (ps[5], ps[7])

            def four(bank, a, b, tr=False):
                for c in range(TILES):
                    o = bank[:, c * P:(c + 1) * P]
                    ins = T.transpose(o, a(c), ident) if tr else T.matmul(o, lhsT=a(c), rhs=b(c), start=True, stop=True)
                return ins

            for hh in HH:
                pe.wait_ge(S("ldb"), at_head(pr, hh))
                if pr:
                    pe.wait_ge(S("s_new_p"), at_tile(0, TILES - 1, hh))
                    pe.wait_ge(S("o_taken"), at_tile(0, TILES - 1, hh))
                four(b0[hh], lambda c: dt(hh, X_)[:, c], lambda c: triu).then_inc(S("grow"), 1)
                four(b1[hh], lambda c: k[hh][:, c], lambda c: k[hh][:, c]).then_inc(S("kk"), 1)
            for hh in HH:
                pe.wait_ge(S("egrow"), at_head(pr, hh))
                four(b0[hh], lambda c: k[hh][:, c], lambda c: q[hh][:, c]).then_inc(S("qk"), 1)
                pe.wait_ge(S("nb_raw"), at_head(pr, hh))
                four(b1[hh], lambda c: k[hh][:, c], None, tr=True).then_inc(S("kt"), 1)
            for hh in HH:
                pe.wait_ge(S("qk_taken"), at_head(pr, hh))
                four(b0[hh], lambda c: v[hh][:, c], None, tr=True).then_inc(S("vt"), 1)
            for n in range(len(LEVELS)):
                for hh in HH:
                    pe.wait_ge(S("as_ready"), at_level(pr, n, hh))
                    if n == 0:
                        pe.wait_ge(S("vt_taken"), at_head(pr, hh))
                    else:
                        pe.wait_ge(S("xy"), 2 * at_level(pr, n - 1, hh) - 1)
                    four(b0[hh], lambda c: dt(hh, W_)[:, c], lambda c: dt(hh, X_)[:, c] if n else ident)\
                        .then_inc(S("ax"), 1)
                if n == 0:
                    continue
                for hh in HH:
                    pe.wait_ge(S("p_ready"), (pr * 6 + n - 1) * 2 + hh + 1)
                    pe.wait_ge(S("xy"), 2 * at_level(pr, n - 1, hh))
                    if n < len(LEVELS) - 1:
                        four(b1[hh], lambda c: dt(hh, Y_)[:, c], lambda c: dt(hh, P_)[:, c]).then_inc(S("xax"), 1)
                    four(b0[hh], lambda c: dt(hh, P_)[:, c], lambda c: dt(hh, Y_)[:, c]).then_inc(S("yay"), 1)
            for c in range(TILES):
                for hh in HH:
                    pe.wait_ge(S("s_new_p" if c else "scaled"), at_tile(pr, c - 1, hh) if c else 2 * at_head(pr, hh))
                    if c == 0:
                        pe.wait_ge(S("xy"), 2 * at_level(pr, len(LEVELS) - 1, hh))
                        pe.wait_ge(S("pst_zero"), 1)
                    else:
                        pe.wait_ge(S("o_taken"), at_tile(pr, c - 1, hh))
                    T.matmul(b0[hh][:, 0:DK], lhsT=k[hh][:, c], rhs=pst[:, 2 * pr + hh], start=True, stop=True)\
                        .then_inc(S("ks"), 1)
                for hh in HH:
                    pe.wait_ge(S("z_ready"), at_tile(pr, c, hh))
                    T.matmul(b1[hh][:, 0:DK], lhsT=dt(hh, Y_)[:, c], rhs=dt(hh, P_)[:, c], start=True, stop=True)\
                        .then_inc(S("yz"), 1)
                for hh in HH:
                    pe.wait_ge(S("u_ready"), at_tile(pr, c, hh))
                    T.matmul(b1[hh][:, 0:DK], lhsT=dt(hh, K_)[:, c], rhs=dt(hh, W_)[:, c], start=True, stop=True)\
                        .then_inc(S("ku"), 1)
                    T.matmul(b0[hh][:, 0:P], lhsT=pst[:, 2 * pr + hh], rhs=q[hh][:, c], start=True, stop=False)
                    T.matmul(b0[hh][:, 0:P], lhsT=dt(hh, W_)[:, c], rhs=dt(hh, QK_)[:, c], start=False, stop=True)\
                        .then_inc(S("o_done"), 1)

        pe.wait_ge(S("o_taken"), at_tile(1, TILES - 1, 1))
        for j in range(CT):
            pe.wait_ge(S("cv_sq"), j + 1)
            for i, src in enumerate((cv[:, j], tmp[:, j % 2])):
                for h, half in enumerate(HALVES):
                    ins = nc.tensor.matmul(ps[4 + 2 * i + h][:, 0:HALF], lhsT=ones[:, 2], rhs=src[:, half],
                                           start=(j == 0), stop=(j == CT - 1))
            ins.then_inc(S("cv_avg"), 1)
        for h in range(HEADS):
            pe.wait_ge(S("rms_sq"), h + 1)
            pe.wait_ge(S("cv_var"), 1)
            if h >= 2:
                pe.wait_ge(S("rms_root"), 2 * (h - 1))
            for i, half in enumerate(HALVES):
                ins = nc.tensor.matmul(ps[4 + 2 * (h % 2) + i][:, 0:HALF], lhsT=ones[:, 1], rhs=sig[:, h % 2, half],
                                       start=True, stop=True)
            ins.then_inc(S("rms_avg"), 1)

        pe.wait_ge(S("rms_root"), 2 * HEADS)
        with pe.Fori(0, 2) as it:
            for m in range(4):
                for gate in range(2):
                    s = 3 * m + gate
                    pe.wait_ge(lo_ready, it * 12 + C_MIX + s + 1)
                    pe.wait_ge(taken[gate], it * 4 + (O_GATE + 2 * m) // 2)
                    gemm(s % RING, out_pair(gate), x, every).then_inc(gemm_done, 1)
                s = 3 * m + 2
                pe.wait_ge(lo_ready, it * 12 + C_MIX + s + 1)
                pe.wait_ge(S("mix_free"), it * 4 + m + 1)
                gemm(s % RING, (ps[4], ps[5]), z, every[0:CT])
                gemm(s % RING, (ps[6], ps[7]), z, every[CT:KB]).then_inc(gemm_done, 1)

        phase(C_WO, O_WO, 8, mixed, [(kb, (S("mixed_lo"), kb + 1)) for kb in range(KB)])
        mem_kbs = [(kb, (S("mem_lo"), kb + 1)) for kb in range(KB)]
        phase(C_MEM, O_MEM, 4, mem, mem_kbs, ((0, N_MEM),))
        ln_average("ln1")
        phase(C_MEM + 4, O_MEM + 4, 4, mem, mem_kbs, ((0, N_MEM),))
        with pe.Fori(0, 2) as g:
            for s in range(RING):
                o = O_MEM + 8 + s
                pe.wait_ge(lo_ready, g * RING + C_MEM + 8 + s + 1)
                pe.wait_ge(taken[o % 2], g * 2 + o // 2)
                for mb in range(2):
                    for kb in range(KB):
                        for j, (a, w) in enumerate(((mem[0], whi), (mem[1], whi), (mem[0], wlo))):
                            ins = nc.tensor.matmul(out_pair(o)[mb][:, 0:P], lhsT=a[:, kb, mb * P:mb * P + P],
                                                   rhs=w[:, s, kb], start=(kb == 0 and j == 0),
                                                   stop=(kb == KB - 1 and j == 2))
                ins.then_inc(gemm_done, 1)
        phase(C_XQ, O_XQ, 8, h1, [(kb, ln("ln1", "out", KB, kb + 1)) for kb in range(KB)])

        pe.wait_ge(taken[0], O_XO // 2)
        pe.wait_ge(taken[1], O_XO // 2)

        def scores(h):
            if h:
                pe.wait_ge(S("att_exp"), 4 * h)
            for t in range(TILES):
                for d in range(2):
                    ins = T.matmul(ps[t // 2][:, (t % 2) * N_MEM:(t % 2 + 1) * N_MEM],
                                   lhsT=aq[:, 2 * h + d, t * P:(t + 1) * P], rhs=mk[:, 2 * h + d],
                                   start=(d == 0), stop=(d == 1))
            ins.then_inc(S("att_sc"), 1)

        def flip(h):
            pe.wait_ge(S("att_p"), h + 1)
            if h:
                pe.wait_ge(S("att_pt"), 2 * h)
            for mb in range(2):
                for t in range(TILES):
                    ins = T.transpose(ps[4 + mb][:, t * P:(t + 1) * P], ap[:, t, mb * P:(mb + 1) * P], ident)
            ins.then_inc(S("att_flip"), 1)

        def values(h):
            pe.wait_ge(S("att_pt"), 2 * (h + 1))
            if h:
                pe.wait_ge(S("ao_lo"), 2 * h)
            for d in range(2):
                for mb in range(2):
                    ins = T.matmul(ps[6 + d][:, :], lhsT=mv[:, mb, (2 * h + d) * P:(2 * h + d + 1) * P],
                                   rhs=apt[:, mb], start=(mb == 0), stop=(mb == 1))
            ins.then_inc(S("att_o"), 1)

        def sample_scores(b):
            pe.wait_ge(S(f"kv_loaded{b % 4}"), 16 * (b // 4 + 1))
            for h in range(X_HEADS):
                for mb in range(2):
                    for d in range(2):
                        a = (2 * h + d) * N_MEM + mb * P
                        col = mb * N_MEM + (b * X_HEADS + h) * DEC_SEQ
                        ins = T.matmul(ps[2][:, col:col + DEC_SEQ], lhsT=kv[:, b % 4, a:a + P],
                                       rhs=aq[:, 2 * h + d, SEQ + 8 * b:SEQ + 8 * b + 8], start=(d == 0), stop=(d == 1))
            ins.then_inc(S("kv_used"), 1)

        scores(0)
        for h in range(X_HEADS):
            sample_scores(2 * h)
            sample_scores(2 * h + 1)
            flip(h)
            if h + 1 < X_HEADS:
                scores(h + 1)
            values(h)
        pe.wait_ge(S("ssc_ready"), 1)
        for g in range(2):
            for mb in range(2):
                ins = T.transpose(ps[3][:, g * N_MEM + mb * P:g * N_MEM + (mb + 1) * P], ssc[:, mb, g * P:(g + 1) * P],
                                  ident)
        ins.then_inc(S("ssc_flip"), 1)
        pe.wait_ge(S("sp_ready"), 1)
        for mb in range(2):
            for g in range(2):
                ins = T.transpose(ps[2][:, mb * N_MEM + g * P:mb * N_MEM + (g + 1) * P], ap[:, g, mb * P:(mb + 1) * P],
                                  ident)
        ins.then_inc(S("sp_flip"), 1)
        pe.wait_ge(S("spt_ready"), 1)
        for b in range(DEC_BATCH):
            i = DEC_BATCH + b
            pe.wait_ge(S(f"kv_loaded{i % 4}"), 16 * (i // 4 + 1))
            for hd in range(2 * X_HEADS):
                for mb in range(2):
                    col = (b * X_HEADS + hd // 2) * DEC_SEQ
                    ins = T.matmul(ps[3][:, hd * SAMPLE + 8 * b:hd * SAMPLE + 8 * b + 8],
                                   lhsT=kv[:, i % 4, mb * D_MODEL + hd * P:mb * D_MODEL + (hd + 1) * P],
                                   rhs=ssc[:, mb, col:col + DEC_SEQ], start=(mb == 0), stop=(mb == 1))
            ins.then_inc(S("kv_used"), 1)

        pe.wait_ge(S("ao_lo"), KB + 1)
        phase(C_XO, O_XO, 8, ao, every)
        ln_average("ln2")
        with pe.Fori(0, QUARTERS) as q:
            for n in range(2 * KB):
                xs = h2 if n < KB else hid
                pe.wait_ge(lo_ready, q * 2 * KB + C_FF + n + 1)
                pe.wait_ge(taken[n % 2], q * KB + (O_FF + n) // 2)
                if n == 0:
                    kbs = [(kb, ln("ln2", "out", KB, kb + 1)) for kb in range(KB)]
                elif n == KB:
                    kbs = [(kb, (S("hid_lo"), q * KB + kb + 1)) for kb in range(KB)]
                else:
                    kbs = every
                gemm(n % RING, out_pair(n), xs, kbs).then_inc(gemm_done, 1)
        ln_average("ln3")

    @block.scalar
    def _(act):
        A_ = nc.scalar.activation

        def split(slot, use):
            act.wait_ge(raw_loaded[slot], use * 16)
            A_(whi[:, slot], raw[:, slot], ACT.Copy).then_inc(hi_ready, 1)

        def store(dst, src):
            act.dma_start(dst, src).then_inc(stored, 16)

        for kb in range(KB):
            if kb % 4 == 0:
                act.wait_ge(S(f"x_loaded{kb // 4}"), 16)
            A_(x[0][:, kb], xraw[:, kb], ACT.Copy).then_inc(S("x_hi"), 1)
        act.wait_ge(S("par_loaded"), 48)
        A_(bdw[0][:], wbd[:], ACT.Copy).then_inc(S("bdw_split"), 1)
        for s in range(RING):
            split(s, 1)

        act.wait_ge(S("q_pad"), 2)
        with act.Fori(0, QT // RING) as g:
            for s in range(RING):
                j = act.snap(g * RING + s)
                lo, hi = out_pair(s)
                act.wait_ge(gemm_done, g * RING + s + 1)
                A_(qraw[:, bass.ds(j, 1), QH:QH + HALF], lo[:, 0:HALF].unsqueeze(1), ACT.Copy)
                A_(qraw[:, bass.ds(j, 1), QH + HALF:RP], hi[:, 0:SEQ - HALF].unsqueeze(1), ACT.Copy)
                A_(qraw[:, bass.ds(j, 1), RP:].rearrange("p o (b t) -> p (o b) t", t=RS)[:, :, QH:],
                   tiled(hi[:, SEQ - HALF:HALF], DEC_SEQ), ACT.Copy).then_inc(taken[s % 2], 1)
                split(s, g + 2)
                act.wait_ge(S("q_conv"), g * (8 * RING) + 8 * (s + 1))
                A_(sig[:, s % 2], qkv[:, bass.ds(j, 1)].rearrange("p o t -> p (o t)"), ACT.Sigmoid)\
                    .then_inc(S("q_sig"), 1)

        act.wait_ge(S("par_loaded"), 48)
        for i in range(CT):
            for gate in (1, 0):
                c = C_GLU + 2 * i + 1 - gate
                if gate:
                    act.wait_ge(gemm_done, c + 1)
                    if i < 2:
                        act.wait_ge(S("q_silu"), QT - 1 + i)
                    else:
                        act.wait_ge(taken[1], O_GLU // 2 + i - 1)
                    for h, half in enumerate(HALVES):
                        ins = A_(sig[:, i % 2, half], out_pair(0)[h][:, 0:HALF], ACT.Sigmoid, bias=pc("b_glu", CT + i))
                    ins.then_inc(taken[0], 1)
                else:
                    act.wait_ge(gemm_done, c + 1)
                split(c % RING, c // RING + 2)

        act.wait_ge(S("dve_own"), 5)
        A_(beta, bd[:, :, 0:4], ACT.Sigmoid).then_inc(S("beta_ready"), 1)
        ch = Chain(act, "act_ld")
        ch(A_(sp1, sp1, ACT.Exp))
        A_(nega, par[:, PAR["a_log"]:PAR["a_log"] + 4], ACT.Exp).then_inc(S("exp_ready"), 1)
        act.wait_ge(S("sp_plus1"), 1)
        A_(sp1, sp1, ACT.Ln).then_inc(S("ln_ready"), 1)

        act.wait_ge(taken[1], O_OG // 2)
        def root(i):
            act.wait_ge(S("l2_sum"), i + 1)
            if i >= 2:
                act.wait_ge(S("l2_done"), i - 1)
            for h, half in enumerate(HALVES):
                A_(tmp[:, i % 2, half], ps[4 + 2 * (i % 2) + h][:, 0:HALF], ACT.Sqrt, bias=eps_l2)\
                    .then_inc(S("l2_root"), 1)
        act.wait_ge(S("consts"), CONSTS)
        for i in range(2 * HEADS):
            if i >= 2:
                root(i - 2)
            A_(sig[:, i % 2], qkv[:, i], ACT.Square).then_inc(S("l2_sq"), 1)
        root(2 * HEADS - 2)
        root(2 * HEADS - 1)

        for i in range(HEADS):
            c, o = C_OG + i, O_OG + i
            act.wait_ge(gemm_done, c + 1)
            if i >= 2:
                act.wait_ge(taken[o % 2], o // 2)
            for h, half in enumerate(HALVES):
                ins = A_(sig[:, i % 2, half], out_pair(o)[h][:, 0:HALF], ACT.Sigmoid)
            ins.then_inc(S("og_sig"), 1)
            split(c % RING, c // RING + 2)

        store(A["qlast"][:], qlast[:])
        act.wait_ge(S("cv_taps"), 2 * CT * CONV_K)
        for j in range(CT):
            store(A["pconv"][:, j], u[:, j, SEQ:UP])
            store(A["sconv"][:, j], u_s(j)[:, :, DEC_SEQ:])

        act.wait_ge(S("s_gd"), 4)
        ch = Chain(act, "act_s")
        ch.step(A_(sw[:, S_E], ps[4][:, 0:4 * SAMPLE], ACT.Exp))
        ch.step(A_(sw[SL, S_D], sw[SL, S_D], ACT.Exp))
        for n in range(1, 3):
            act.wait_ge(S("s_ax"), n + 1)
            A_(sw[SL, S_P], ps[4][SL, 0:4 * SAMPLE], ACT.Copy).then_inc(S("s_p"), 1)
        act.wait_ge(S("s_ztt"), 1)
        A_(sz[SL], ps[7][SL, :], ACT.Copy).then_inc(S("s_z"), 1)
        act.wait_ge(S("s_o"), 1)
        A_(qkv[:, 2 * HEADS:, ST], tiled(ps[5][:, 0:4 * SAMPLE], SAMPLE), ACT.Copy).then_inc(S("s_otaken"), 1)
        act.wait_ge(S("s_new"), 3 * HEADS)
        store(A["sdelta_out"][:], sst[:])

        for pr in range(2):
            b0 = (ps[4], ps[6])
            for hh in range(2):
                act.wait_ge(S("gd"), TILES * at_head(pr, hh))
                A_(dl[:, hh, P_], b0[hh][:, :], ACT.Exp).then_inc(S("egrow"), 1)
                A_(dl[:, hh, W_], dl[:, hh, W_], ACT.Exp).then_inc(S("decay"), 1)
            for hh in range(2):
                act.wait_ge(S("vt"), at_head(pr, hh))
                A_(dl[:, hh, V_], b0[hh][:, :], ACT.Copy).then_inc(S("vt_taken"), 1)
            for n in range(1, len(LEVELS)):
                for hh in range(2):
                    act.wait_ge(S("ax"), at_level(pr, n, hh))
                    A_(dl[:, hh, P_], b0[hh][:, :], ACT.Copy).then_inc(S("p_ready"), 1)
            for c in range(TILES):
                for hh in range(2):
                    act.wait_ge(S("o_done"), at_tile(pr, c, hh))
                    A_(qkv[:, 2 * HEADS + 2 * pr + hh, c * P:(c + 1) * P], b0[hh][:, 0:P], ACT.Copy)\
                        .then_inc(S("o_taken"), 1)
        act.wait_ge(S("s_new_p"), at_tile(1, TILES - 1, 1))
        store(A["pdelta_out"][:], pst[:])

        for j in range(CT):
            if j == 0:
                act.wait_ge(S("o_taken"), at_tile(1, TILES - 1, 1))
            if j >= 2:
                act.wait_ge(S("cv_avg"), j - 1)
            A_(tmp[:, j % 2], cv[:, j], ACT.Square).then_inc(S("cv_sq"), 1)
        act.wait_ge(S("cv_var"), 1)
        A_(nrm[:, 1], nrm[:, 1], ACT.Sqrt, bias=eps_ln).then_inc(S("cv_root"), 1)
        def rms_root(h):
            act.wait_ge(S("rms_avg"), h + 1)
            if h >= 2:
                act.wait_ge(S("rms_mul"), h - 1)
            for i, half in enumerate(HALVES):
                A_(tmp[:, h % 2, half], ps[4 + 2 * (h % 2) + i][:, 0:HALF], ACT.Sqrt, bias=eps_l2)\
                    .then_inc(S("rms_root"), 1)
        for h in range(HEADS):
            if h >= 2:
                rms_root(h - 2)
            A_(sig[:, h % 2], qkv[:, 2 * HEADS + h], ACT.Square).then_inc(S("rms_sq"), 1)
        rms_root(HEADS - 2)
        rms_root(HEADS - 1)
        act.wait_ge(stored, 16 * (3 + 2 * CT))
        for j in range(CT):
            act.wait_ge(S("cv_norm"), j + 1)
            if j == 0:
                act.wait_ge(S("rms_avg"), HEADS)
            if j >= 2:
                act.wait_ge(S("cv_silu"), j - 1)
            A_(sig[:, j % 2], cv[:, j], ACT.Sigmoid).then_inc(S("cv_sig"), 1)
            act.wait_ge(S("cv_silu"), j + 1)
            A_(z[0][:, j], cv[:, j], ACT.Copy).then_inc(S("z_hi"), 1)
        for h in range(HEADS):
            act.wait_ge(S("rms_out"), h + 1)
            A_(z[0][:, CT + h], qkv[:, 2 * HEADS + h], ACT.Copy).then_inc(S("z_hi"), 1)

        act.wait_ge(S("z_lo"), KB)
        with act.Fori(0, 2) as it:
            for m in range(4):
                for gate, dst in enumerate((ga, gb)):
                    s = 3 * m + gate
                    act.wait_ge(gemm_done, it * 12 + C_MIX + s + 1)
                    act.wait_ge(S("mix_free"), it * 4 + m + (1 if m < 2 else 0) if m < 2 else it * 4 + m)
                    for h, half in enumerate(HALVES):
                        ins = A_(dst[:, m % 2, half], out_pair(gate)[h][:, 0:HALF], ACT.Sigmoid)
                    ins.then_inc(taken[gate], 1)
                    split(s % RING, it * 3 + (C_MIX + s) // RING + 2)
                s = 3 * m + 2
                act.wait_ge(gemm_done, it * 12 + C_MIX + s + 1)
                split(s % RING, it * 3 + (C_MIX + s) // RING + 2)
                mm = act.snap(it * 4 + m)
                act.wait_ge(S("mixed"), mm + 1)
                A_(mixed[0][:, bass.ds(mm, 1)], mx[:, m % 2, 0:1], ACT.Copy).then_inc(S("mixed_hi"), 1)

        def squares(name, c0):
            with act.Fori(0, 2) as g:
                for s in range(RING):
                    j = act.snap(g * RING + s)
                    act.wait_ge(gemm_done, g * RING + c0 + s + 1)
                    split(s, g + c0 // RING + 2)
                    act.wait_ge(*ln(name, "res", KB, j + 1))
                    A_(lnt[:, s % 2], res[:, bass.ds(j, 1)].rearrange("p o t -> p (o t)"), ACT.Square)\
                        .then_inc(S("ln_sq"), 1)

        def ln_root(name):
            act.wait_ge(*ln(name, "var", 1, 1))
            A_(lns[:, 1], lns[:, 1], ACT.Sqrt, bias=eps_ln).then_inc(S("ln_root"), 1)

        def ln_affine(name, g, b, j, out):
            act.wait_ge(*ln(name, "norm", 2 * KB, 2 * (j + 1)))
            A_(res[:, j], res[:, j], ACT.Identity, bias=pc(b, j), scale=pc(g, j)).then_inc(S("ln_aff"), 1)
            act.wait_ge(*ln(name, "aff", KB, j + 1))
            if out is not None:
                A_(out[0][:, j], res[:, j], ACT.Copy).then_inc(S("ln_hi"), 1)

        squares("ln1", C_WO)
        act.wait_ge(S("mem_loaded"), 16)
        for kb in range(KB):
            A_(mem[0][:, kb], memraw[:, kb], ACT.Copy).then_inc(S("mem_hi"), 1)
        for i in range(2 * KB):
            c, o = C_MEM + i, O_MEM + i
            act.wait_ge(gemm_done, c + 1)
            if i < KB:
                A_(mk[:, i], out_pair(o)[0][:, 0:N_MEM], ACT.Copy).then_inc(taken[o % 2], 1)
            else:
                for mb in range(2):
                    ins = A_(mv[:, mb, (i - KB) * P:(i - KB + 1) * P], out_pair(o)[mb][:, 0:P], ACT.Copy)
                ins.then_inc(taken[o % 2], 1)
            split(c % RING, c // RING + 2)
            if i == 4:
                ln_root("ln1")
            if 5 <= i < 5 + KB:
                ln_affine("ln1", "g1", "b1", i - 5, h1)
        act.wait_ge(taken[0], (O_MEM + 2 * KB) // 2)
        act.wait_ge(taken[1], (O_MEM + 2 * KB) // 2)
        store(A["mk"][:], mk[:])
        store(A["mv"][:], mv[:])

        act.wait_ge(*ln("ln1", "out", KB, KB))
        with act.Fori(0, 2) as g:
            for s in range(RING):
                j = act.snap(g * RING + s)
                act.wait_ge(gemm_done, g * RING + C_XQ + s + 1)
                for h, half in enumerate(HALVES):
                    ins = A_(aq[:, bass.ds(j, 1), half], out_pair(s)[h][:, 0:HALF].unsqueeze(1), ACT.Copy,
                             scale=X_DIM ** -0.5)
                ins.then_inc(taken[s % 2], 1)
                split(s, g + C_XQ // RING + 2)

        for h in range(X_HEADS):
            act.wait_ge(S("att_max"), 3 * (h + 1))
            if h:
                act.wait_ge(S("att_flip"), h)
            for t in range(TILES):
                A_(ap[:, t], ps[t // 2][:, (t % 2) * N_MEM:(t % 2 + 1) * N_MEM], ACT.Exp, bias=amax[:, t:t + 1],
                   accum_out=asum[:, t:t + 1]).then_inc(S("att_exp"), 1)
            act.wait_ge(S("att_flip"), h + 1)
            if h:
                act.wait_ge(S("att_o"), h)
            for mb in range(2):
                A_(apt[:, mb], ps[4 + mb][:, :], ACT.Copy).then_inc(S("att_pt"), 1)
            if h == X_HEADS - 1:
                act.wait_ge(S("kv_used"), DEC_BATCH)
                A_(ssc[:], ps[2][:, :].rearrange("p (m c) -> p m c", m=2), ACT.Copy).then_inc(S("ssc_ready"), 1)
            act.wait_ge(S("att_o"), h + 1)
            for d in range(2):
                A_(ao[0][:, 2 * h + d, PT], ps[6 + d][:, :], ACT.Copy).then_inc(S("ao_hi"), 1)
        act.wait_ge(S("att_max"), 3 * X_HEADS + 2)
        for g in range(2):
            A_(ap[:, g], ps[3][:, g * N_MEM:(g + 1) * N_MEM], ACT.Exp, bias=amax[:, g:g + 1],
               accum_out=asum[:, g:g + 1]).then_inc(S("att_exp"), 1)
        act.wait_ge(S("sp_flip"), 1)
        A_(ssc[:], ps[2][:, :].rearrange("p (m c) -> p m c", m=2), ACT.Copy).then_inc(S("spt_ready"), 1)
        act.wait_ge(S("kv_used"), 2 * DEC_BATCH)
        A_(ao[0][:, :, ST], tiled(ps[3][:, :], SAMPLE), ACT.Copy).then_inc(S("ao_hi"), 1)

        squares("ln2", C_XO)
        ln_root("ln2")
        for j in range(KB):
            ln_affine("ln2", "g2", "b2", j, h2)

        def quarter(q, last=False):
            for n in range(2 * KB):
                c = C_FF + n
                act.wait_ge(gemm_done, q * (2 * KB) + c + 1)
                if n < KB:
                    if n >= 2:
                        act.wait_ge(S("hid_lo"), q * KB + n - 1)
                    for h, half in enumerate(HALVES):
                        ins = A_(ht[:, n % 2, half], out_pair(n)[h][:, 0:HALF], ACT.Relu)
                    ins.then_inc(taken[n % 2], 1)
                    act.wait_ge(taken[n % 2], q * KB + (O_FF + n) // 2 + 1)
                    A_(hid[0][:, n], ht[:, n % 2], ACT.Square).then_inc(S("hid_hi"), 1)
                if not (last and n >= 2 * KB - RING):
                    split(n % RING, q * (2 * KB // RING) + c // RING + 2)
                if last and n >= KB:
                    j = n - KB
                    act.wait_ge(S("acc"), q * KB + j + 1)
                    act.wait_ge(taken[j % 2], q * KB + (O_FF + KB + j) // 2 + 1)
                    A_(lnt[:, j % 2], res[:, j], ACT.Square).then_inc(S("ln_sq"), 1)
        act.wait_ge(S("acc_ready"), KB)
        act.wait_ge(stored, 16 * (5 + 2 * CT))
        with act.Fori(0, QUARTERS - 1) as q:
            quarter(q)
        quarter(QUARTERS - 1, True)
        ln_root("ln3")
        for j in range(KB):
            ln_affine("ln3", "g3", "b3", j, None)
            store(A["yT"][:, j], res[:, j])

    @block.vector
    def _(dve):
        V = nc.vector

        for kb in range(KB):
            dve.wait_ge(S("x_hi"), kb + 1)
            V.tensor_tensor(x[1][:, kb], xraw[:, kb], x[0][:, kb].bitcast(f32), sub).then_inc(S("x_lo"), 1)
        dve.wait_ge(S("bdw_split"), 1)
        V.tensor_tensor(bdw[1][:], wbd[:], bdw[0][:].bitcast(f32), sub).then_inc(S("bdw_split"), 1)
        dve.wait_ge(S("x_lo"), KB)
        dve.wait_ge(S("par_loaded"), 48)
        V.memset(qraw[:, :, 0:QH], 0.0).then_inc(S("q_pad"), 1)
        V.tensor_copy(qraw[:, :, RP:].rearrange("p j (b t) -> p j b t", t=RS)[:, :, :, 0:QH],
                      qhist[:].rearrange("p j (b t) -> p j b t", t=QH)).then_inc(S("q_pad"), 1)
        own = ch = Chain(dve, "dve_own")
        dve.wait_ge(S("par_loaded"), 48)
        ch(V.memset(bd, 0.0))
        dve.wait_ge(S("bd_done"), 1)
        V.tensor_copy(bd[:, 0:TILES], ps[4][:, 0:32].rearrange("p (t c) -> p t c", c=8))
        ch(V.tensor_copy(bd[SL, TILES], ps[4][SL, 32:40]))
        ch(V.tensor_tensor(sp0, bd[:, :, 4:8], rep(par[:, PAR["dt_bias"]:PAR["dt_bias"] + 4], 5), add))
        ch(V.tensor_scalar(sp1, sp0, -1.0, None, mul))
        ch(V.tensor_tensor(sp1, sp0, sp1, ALU.min))

        def conv_taps(sem, ch, width, weight, src_p, src_s, dst_p, dst_s, taps, bias=None):
            for k in taps:
                for src, dst in ((src_p, dst_p), (src_s, dst_s)):
                    ch.wait(1)
                    w = weight(k)
                    if k == 0:
                        ins = V.tensor_scalar(dst, src(k), w, bias, mul, add if bias is not None else ALU.bypass)
                    else:
                        ins = V.scalar_tensor_tensor(dst, src(k), w, dst, mul, add)
                    ch.step(ins)

        with dve.Fori(0, QT // RING) as g:
            for s in range(RING):
                j = dve.snap(g * RING + s)
                ch = Chain(dve, "q_conv", g * (8 * RING) + 8 * s)
                dve.wait_ge(taken[s % 2], g * 2 + s // 2 + 1)
                row = qraw[:, bass.ds(j, 1)]
                out = qkv[:, bass.ds(j, 1)]
                wcol = dve.snap(j * SHORT_K + PAR["w_short"])
                conv_taps(None, ch, SHORT_K, lambda k: par[:, bass.ds(wcol + k, 1)],
                          lambda k: row[:, :, k:k + SEQ].rearrange("p o t -> p (o t)"),
                          lambda k: row[:, :, RP:].rearrange("p o (b t) -> p (o b) t", t=RS)[:, :, k:k + DEC_SEQ],
                          out[:, :, PT].rearrange("p o t -> p (o t)"),
                          out[:, :, ST].rearrange("p o (b t) -> p (o b) t", t=DEC_SEQ), range(SHORT_K))
                ch.wait()
                dve.wait_ge(S("q_sig"), g * RING + s + 1)
                o = out.rearrange("p o t -> p (o t)")
                V.tensor_tensor(o, o, sig[:, s % 2], mul).then_inc(S("q_silu"), 1)
        V.tensor_copy(qlast[:, :, 0:QH], qraw[:, :, SEQ:RP]).then_inc(S("q_last"), 1)
        V.tensor_copy(qlast[:, :, QH:].rearrange("p j (b t) -> p j b t", t=QH),
                      qraw[:, :, RP:].rearrange("p j (b t) -> p j b t", t=RS)[:, :, :, DEC_SEQ:]).then_inc(S("qraw_free"), 1)

        dve.wait_ge(S("consts"), CONSTS)
        dve.wait_ge(S("cst_loaded"), 16 * (2 + CT))
        chc = Chain(dve, "cv_taps")
        todo = [(j, k) for j in range(CT) for k in range(CONV_K)]

        def wide_taps(n):
            for j, k in todo[:n]:
                conv_taps(None, chc, CONV_K, lambda kk: pc("w_dw", j * CONV_K + kk),
                          lambda kk: u[:, j, kk:kk + SEQ], lambda kk: u_s(j)[:, :, kk:kk + DEC_SEQ],
                          cv[:, j, PT], tiled(cv[:, j, ST], DEC_SEQ), [k], bias=pc("b_dw", j))
            del todo[:n]

        for i in range(CT):
            dve.wait_ge(taken[0], O_GLU // 2 + i + 1)
            dve.wait_ge(gemm_done, C_GLU + 2 * i + 2)
            lo, hi = out_pair(1)
            bias = pc("b_glu", i)
            V.scalar_tensor_tensor(u[:, i, CH:CH + HALF], lo[:, 0:HALF], bias, sig[:, i % 2, 0:HALF], add, mul)
            V.scalar_tensor_tensor(u[:, i, CH + HALF:UP], hi[:, 0:SEQ - HALF], bias, sig[:, i % 2, HALF:SEQ], add, mul)
            V.scalar_tensor_tensor(u_s(i)[:, :, CH:], tiled(hi[:, SEQ - HALF:HALF], DEC_SEQ), bias,
                                   tiled(sig[:, i % 2, ST], DEC_SEQ), add, mul).then_inc(taken[1], 1)
            dve.wait_ge(taken[1], O_GLU // 2 + i + 1)
            if i < CT - 1:
                wide_taps(13)
        ch = own
        dve.wait_ge(S("exp_ready"), 1)
        V.tensor_scalar(sp1, sp1, 1.0, None, add).then_inc(S("sp_plus1"), 1)
        ch(V.tensor_scalar(nega, nega, -1.0, None, mul))
        ch(V.tensor_scalar(sp0, sp0, 0.0, None, ALU.max))
        dve.wait_ge(S("ln_ready"), 1)
        ch(V.tensor_tensor(sp0, sp0, sp1, add))
        V.tensor_tensor(ld, sp0, rep(nega, 5), mul).then_inc(S("ld_ready"), 1)
        dve.wait_ge(S("g_done"), 1)
        V.tensor_copy(gcol[SL, TILES], ps[4][SL, 80:84])
        V.tensor_copy(gcol[:, 0:TILES], ps[4][:, 64:80].rearrange("p (t c) -> p t c", c=4))\
            .then_inc(S("gcol_ready"), 1)
        for i in range(2 * HEADS):
            dve.wait_ge(S("l2_root"), 2 * (i + 1))
            ch(V.reciprocal(tmp[:, i % 2], tmp[:, i % 2]))
            V.scalar_tensor_tensor(qkv[:, i], tmp[:, i % 2], DK ** -0.5 if i < HEADS else 1.0, qkv[:, i], mul, mul)\
                .then_inc(S("l2_done"), 1)
        for i in range(HEADS):
            dve.wait_ge(S("og_sig"), i + 1)
            for h, half in enumerate(HALVES):
                ins = V.tensor_tensor(sgate[:, i, half], out_pair(O_OG + i)[h][:, 0:HALF], sig[:, i % 2, half], mul)
            ins.then_inc(taken[(O_OG + i) % 2], 1)
            wide_taps(8)
        wide_taps(len(todo))
        chc.wait()

        dve.wait_ge(S("gcol_ready"), 1)
        dve.wait_ge(S("ld_ready"), 1)
        dve.wait_ge(S("l2_done"), 2 * HEADS)
        dve.wait_ge(stored, 16 * (1 + 2 * CT))
        dve.wait_ge(S("beta_ready"), 1)
        V.tensor_copy(sld[SL], bc(ld[SL, TILES], DK)).then_inc(S("sld_ready"), 1)
        V.memset(pst[:], 0.0).then_inc(S("pst_zero"), 1)
        dve.wait_ge(S("s_grow"), 1)
        for h in range(HEADS):
            V.tensor_scalar(sw[SL, S_D, h], ps[4][SL, h * SAMPLE:(h + 1) * SAMPLE], gcol[SL, TILES, h:h + 1], 0.0,
                            sub, ALU.min).then_inc(S("s_gd"), 1)
        dve.wait_ge(S("act_s"), 2)
        D, E = sw[SL, S_D], sw[:, S_E]
        ch(V.tensor_tensor(D, D, rep(triu8[SL], HEADS), mul))
        ch.step(V.tensor_reduce(stail[SL], D.rearrange("p h (b t) -> p h b t", t=DEC_SEQ)[:, :, :, DEC_SEQ - 1], X, add))
        ch.step(V.tensor_copy(seglast, E.rearrange("p h (b t) -> p h b t", t=DEC_SEQ)[:, :, :, DEC_SEQ - 1]))
        dve.wait_ge(S("s_kk"), 1)
        ch(V.tensor_tensor(sw[SL, S_NB], tiled(ps[5][SL, 0:256], SAMPLE), D, mul))
        ch(V.tensor_tensor(sw[SL, S_NB], sw[SL, S_NB], bc(beta[SL, TILES], SAMPLE), mul))
        ch.step(V.tensor_tensor(sw[SL, S_QK], tiled(ps[5][SL, 256:512], SAMPLE), D, mul))
        dve.wait_ge(S("s_kt"), 1)
        ch(V.tensor_tensor(skt[SL], tiled(ps[6][SL, :]), bc(stail[SL], DK), mul))
        V.tensor_tensor(qkv[:, 0:HEADS, ST], qkv[:, 0:HEADS, ST], E, mul).then_inc(S("s_scaled"), 1)
        V.tensor_tensor(qkv[:, HEADS:2 * HEADS, ST], qkv[:, HEADS:2 * HEADS, ST], E, mul).then_inc(S("s_scaled"), 1)
        for n in range(3):
            if n:
                dve.wait_ge(S("s_ax"), n)
                dve.wait_ge(S("s_xy"), 2 * n)
            V.tensor_tensor(sw[SL, S_W], sw[SL, S_NB], rep(lmask[SL, n, SL], HEADS), mul).then_inc(S("s_as"), 1)
            if n == 0:
                dve.wait_ge(S("s_as"), 1)
                dve.wait_ge(S("s_ax"), 1)
                V.tensor_tensor(sw[SL, S_X], rep(ident[SL, SL], HEADS), tiled(ps[4][SL, 0:256], SAMPLE), sub)\
                    .then_inc(S("s_xy"), 1)
                V.tensor_tensor(sw[SL, S_Y], rep(ident[SL, SL], HEADS), sw[SL, S_W], sub).then_inc(S("s_xy"), 1)
            else:
                dve.wait_ge(S("s_xax"), n)
                for i, k in enumerate((S_X, S_Y)):
                    V.tensor_tensor(sw[SL, k], sw[SL, k], tiled(ps[5][SL, 256 * i:256 * (i + 1)], SAMPLE), sub)\
                        .then_inc(S("s_xy"), 1)
                dve.wait_ge(S("s_xy"), 2 * (n + 1))
        dve.wait_ge(S("s_ks"), 1)
        V.tensor_tensor(szt[:], qkv[:, 2 * HEADS:, ST], tiled(ps[6][:, 0:256], SAMPLE), sub).then_inc(S("s_zt"), 1)
        dve.wait_ge(S("s_yz"), 1)
        V.tensor_tensor(su[SL], tiled(ps[4][SL, :]), bc(beta[SL, TILES], DK), mul).then_inc(S("s_u"), 1)
        for h in range(HEADS):
            if h >= 2:
                dve.wait_ge(S("s_ds"), h - 1)
            V.tensor_tensor(sktm[SL, h % 2], rep(skt[SL, h], DEC_BATCH), bc(same8[SL], DK), mul).then_inc(S("s_ktm"), 1)
            if h == 0:
                dve.wait_ge(S("s_o"), 1)
            V.tensor_tensor(sst[:, h], sst[:, h], bc(seglast[:, h], DK), mul).then_inc(S("s_new"), 1)
            dve.wait_ge(S("s_new"), 3 * h + 1)
            dve.wait_ge(S("s_ds"), h + 1)
            for i in range(2):
                half = sst[:, h, 4 * i:4 * i + 4]
                V.tensor_tensor(half, half, tiled(ps[6 + i][:, :]), add).then_inc(S("s_new"), 1)

        dve.wait_ge(S("s_otaken"), 1)
        for pr in range(2):
            b0, b1 = (ps[4], ps[6]), (ps[5], ps[7])
            for hh in range(2):
                if pr:
                    dve.wait_ge(S("o_done"), at_tile(0, TILES - 1, hh))
                    dve.wait_ge(S("ku"), at_tile(0, TILES - 1, hh))
                V.tensor_copy(dt(hh, X_), bc(ld[:, 0:TILES, 2 * pr + hh], P)).then_inc(S("ldb"), 1)
            for hh in range(2):
                h = 2 * pr + hh
                dve.wait_ge(S("grow"), at_head(pr, hh))
                for c in range(TILES):
                    V.tensor_scalar(dt(hh, W_)[:, c], b0[hh][:, c * P:(c + 1) * P], gcol[:, c, h:h + 1], 0.0, sub,
                                    ALU.min).then_inc(S("gd"), 1)
            for hh in range(2):
                h = 2 * pr + hh
                dve.wait_ge(S("decay"), at_head(pr, hh))
                D, E = dt(hh, W_), dt(hh, P_)
                ch(V.tensor_tensor(D, D, rep(triu, TILES), mul))
                ch.step(V.tensor_copy(etail[:, hh], D[:, :, P - 1]))
                ch.step(V.tensor_copy(eglast[:, hh], E[:, :, P - 1]))
                dve.wait_ge(S("kk"), at_head(pr, hh))
                V.tensor_tensor(dt(hh, NB_), tiled(b1[hh][:, :]), D, mul).then_inc(S("nb_raw"), 1)
                dve.wait_ge(S("nb_raw"), at_head(pr, hh))
                ch.step(V.tensor_tensor(dt(hh, NB_), dt(hh, NB_), bc(beta[:, 0:TILES, h], P), mul))
                dve.wait_ge(S("qk"), at_head(pr, hh))
                V.tensor_tensor(dt(hh, QK_), tiled(b0[hh][:, :]), D, mul).then_inc(S("qk_taken"), 1)
            for hh in range(2):
                h = 2 * pr + hh
                dve.wait_ge(S("kt"), at_head(pr, hh))
                ch.wait()
                ch.step(V.tensor_tensor(dt(hh, K_), tiled(b1[hh][:, :]), bc(etail[:, hh], P), mul))
                for w in (HEADS + h, h):
                    V.tensor_tensor(qkv[:, w, PT], qkv[:, w, PT], dl[:, hh, P_], mul).then_inc(S("scaled"), 1)
            for n in range(len(LEVELS)):
                for hh in range(2):
                    if n:
                        dve.wait_ge(S("ax"), at_level(pr, n - 1, hh))
                        dve.wait_ge(S("xy"), 2 * at_level(pr, n - 1, hh))
                    else:
                        dve.wait_ge(S("qk_taken"), at_head(pr, hh))
                    V.tensor_tensor(dt(hh, W_), dt(hh, NB_), rep(lmask[:, n], TILES), mul).then_inc(S("as_ready"), 1)
                for hh in range(2):
                    if n == 0:
                        dve.wait_ge(S("as_ready"), at_level(pr, n, hh))
                        dve.wait_ge(S("ax"), at_level(pr, n, hh))
                        V.tensor_tensor(dt(hh, X_), rep(ident, TILES), tiled(b0[hh][:, :]), sub).then_inc(S("xy"), 1)
                        V.tensor_tensor(dt(hh, Y_), rep(ident, TILES), dt(hh, W_), sub).then_inc(S("xy"), 1)
                        continue
                    dve.wait_ge(S("xy"), 2 * at_level(pr, n - 1, hh))
                    if n < len(LEVELS) - 1:
                        dve.wait_ge(S("xax"), (pr * 5 + n - 1) * 2 + hh + 1)
                        V.tensor_tensor(dt(hh, X_), dt(hh, X_), tiled(b1[hh][:, :]), sub).then_inc(S("xy"), 1)
                        dve.wait_ge(S("yay"), (pr * 6 + n - 1) * 2 + hh + 1)
                        V.tensor_tensor(dt(hh, Y_), dt(hh, Y_), tiled(b0[hh][:, :]), sub).then_inc(S("xy"), 1)
                    else:
                        dve.wait_ge(S("yay"), (pr * 6 + n - 1) * 2 + hh + 1)
                        V.tensor_tensor(dt(hh, Y_), dt(hh, Y_), tiled(b0[hh][:, :]), sub).then_inc(S("xy"), 2)
            for c in range(TILES):
                for hh in range(2):
                    dve.wait_ge(S("ks"), at_tile(pr, c, hh))
                    V.tensor_tensor(dt(hh, P_)[:, c], dt(hh, V_)[:, c], b0[hh][:, 0:DK], sub).then_inc(S("z_ready"), 1)
                for hh in range(2):
                    dve.wait_ge(S("yz"), at_tile(pr, c, hh))
                    V.tensor_scalar(dt(hh, W_)[:, c], b1[hh][:, 0:DK], beta[:, c, 2 * pr + hh:2 * pr + hh + 1], None,
                                    mul).then_inc(S("u_ready"), 1)
                for hh in range(2):
                    state = pst[:, 2 * pr + hh]
                    dve.wait_ge(S("ku"), at_tile(pr, c, hh))
                    dve.wait_ge(S("o_done"), at_tile(pr, c, hh))
                    V.scalar_tensor_tensor(state, state, eglast[:, hh, c:c + 1], b1[hh][:, 0:DK], mul, add)\
                        .then_inc(S("s_new_p"), 1)

        dve.wait_ge(S("cv_avg"), CT)

        def variance(ch, mean, var, work):
            for h, half in enumerate(HALVES):
                ch(V.tensor_copy(mean[:, half], ps[4 + h][:, 0:HALF]))
            ch(V.tensor_tensor(work, mean, mean, mul))
            for h, half in enumerate(HALVES):
                ch(V.tensor_tensor(var[:, half], ps[6 + h][:, 0:HALF], work[:, half], sub))
            return V.tensor_scalar(var, var, 0.0, None, ALU.max)

        variance(ch, nrm[:, 0], nrm[:, 1], tmp[:, 0]).then_inc(S("cv_var"), 1)
        dve.wait_ge(S("cv_root"), 1)
        ch(V.reciprocal(nrm[:, 1], nrm[:, 1]))
        for j in range(CT):
            c = cv[:, j]
            ch(V.tensor_tensor(c, c, nrm[:, 0], sub))
            ch(V.tensor_tensor(c, c, nrm[:, 1], mul))
            V.tensor_scalar(c, c, pc("cg", j), pc("cb", j), mul, add).then_inc(S("cv_norm"), 1)
        for h in range(HEADS):
            o, t = qkv[:, 2 * HEADS + h], tmp[:, h % 2]
            dve.wait_ge(S("rms_root"), 2 * (h + 1))
            ch(V.reciprocal(t, t))
            ch(V.tensor_tensor(o, o, t, mul))
            V.engine_nop().then_inc(S("rms_mul"), 1)
            V.scalar_tensor_tensor(o, o, pc("dng"), sgate[:, h], mul, mul).then_inc(S("rms_out"), 1)
        for j in range(CT):
            dve.wait_ge(S("cv_norm"), j + 1)
            dve.wait_ge(S("cv_sig"), j + 1)
            V.tensor_tensor(cv[:, j], cv[:, j], sig[:, j % 2], mul).then_inc(S("cv_silu"), 1)
            dve.wait_ge(S("z_hi"), j + 1)
            V.tensor_tensor(z[1][:, j], cv[:, j], z[0][:, j].bitcast(f32), sub).then_inc(S("z_lo"), 1)
        for h in range(HEADS):
            dve.wait_ge(S("z_hi"), CT + h + 1)
            V.tensor_tensor(z[1][:, CT + h], qkv[:, 2 * HEADS + h], z[0][:, CT + h].bitcast(f32), sub)\
                .then_inc(S("z_lo"), 1)
        dve.wait_ge(S("z_lo"), KB)
        V.engine_nop().then_inc(S("mix_free"), 1)

        with dve.Fori(0, 2) as it:
            for m in range(4):
                mm = dve.snap(it * 4 + m)
                ch = Chain(dve, "dve_mix", it * 8 + 2 * m)
                dve.wait_ge(gemm_done, it * 12 + C_MIX + 3 * m + 3)
                dve.wait_ge(taken[1], it * 4 + O_GATE // 2 + m + 1)
                dve.wait_ge(taken[0], it * 4 + O_GATE // 2 + m + 1)
                a, b = mx[:, m % 2, 0], mx[:, m % 2, 1]
                for h, half in enumerate(HALVES):
                    ins = V.tensor_tensor(a[:, half], ps[4 + h][:, 0:HALF], ga[:, m % 2, half], mul)
                    if h == 0:
                        ch.step(ins)
                ch.step(ins)
                V.tensor_tensor(b[:, HALVES[0]], ps[6][:, 0:HALF], gb[:, m % 2, HALVES[0]], mul)
                V.tensor_tensor(b[:, HALVES[1]], ps[7][:, 0:HALF], gb[:, m % 2, HALVES[1]], mul)\
                    .then_inc(S("mix_free"), 1)
                ch.wait()
                dve.wait_ge(S("mix_free"), mm + 2)
                V.tensor_tensor(a, a, b, add).then_inc(S("mixed"), 1)
                dve.wait_ge(S("mixed_hi"), mm + 1)
                V.tensor_tensor(mixed[1][:, bass.ds(mm, 1)], mx[:, m % 2, 0:1],
                                mixed[0][:, bass.ds(mm, 1)].bitcast(f32), sub).then_inc(S("mixed_lo"), 1)

        def residual(name, c0, o0, old):
            V.memset(lns[:], 0.0).then_inc(S("ln_zero"), 1)
            dve.wait_ge(*ln(name, "zero", 1, 1))
            with dve.Fori(0, 2) as g:
                for s in range(RING):
                    j = dve.snap(g * RING + s)
                    r = res[:, bass.ds(j, 1)]
                    ch = Chain(dve, name + "_t", g * RING + s)
                    dve.wait_ge(gemm_done, g * RING + c0 + s + 1)
                    for h, half in enumerate(HALVES):
                        ins = V.scalar_tensor_tensor(r[:, :, half], old[0][:, bass.ds(j, 1), half].bitcast(f32), ALPHA,
                                                     out_pair(s)[h][:, 0:HALF].unsqueeze(1), mul, add)
                        if h == 0:
                            ch.step(ins)
                    ins.then_inc(taken[s % 2], 1)
                    ch.wait()
                    dve.wait_ge(taken[s % 2], g * 2 + (o0 + s) // 2 + 1)
                    V.scalar_tensor_tensor(r, old[1][:, bass.ds(j, 1)].bitcast(f32), ALPHA, r, mul, add)\
                        .then_inc(S("ln_res"), 1)
                    dve.wait_ge(*ln(name, "res", KB, j + 1))
                    V.tensor_tensor(lns[:, 0:1], lns[:, 0:1], r, add).then_inc(S("ln_sum"), 1)
                    dve.wait_ge(*ln(name, "sq", KB, j + 1))
                    V.tensor_tensor(lns[:, 1], lns[:, 1], lnt[:, s % 2], add).then_inc(S("ln_sum"), 1)
                    dve.wait_ge(*ln(name, "sum", 2 * KB, g * (2 * RING) + 2 * s + 2))

        def normalise(name, out, scale_after=None):
            ch = own
            dve.wait_ge(*ln(name, "avg", 1, 1))
            variance(ch, lns[:, 0], lns[:, 1], lnt[:, 0]).then_inc(S("ln_var"), 1)
            dve.wait_ge(*ln(name, "root", 1, 1))
            ch(V.reciprocal(lns[:, 1], lns[:, 1]))

            def lo(j):
                dve.wait_ge(*ln(name, "hi", KB, j + 1))
                V.tensor_tensor(out[1][:, j], res[:, j], out[0][:, j].bitcast(f32), sub).then_inc(S("ln_out"), 1)
                if scale_after:
                    dve.wait_ge(*ln(name, "out", KB, j + 1))
                    V.tensor_scalar(res[:, j], res[:, j], scale_after, None, mul).then_inc(S("acc_ready"), 1)

            for j in range(KB):
                V.tensor_tensor(res[:, j], res[:, j], lns[:, 0], sub).then_inc(S("ln_norm"), 1)
                dve.wait_ge(*ln(name, "norm", 2 * KB, 2 * j + 1))
                V.tensor_tensor(res[:, j], res[:, j], lns[:, 1], mul).then_inc(S("ln_norm"), 1)
                if out is not None and j:
                    lo(j - 1)
            if out is not None:
                lo(KB - 1)

        residual("ln1", C_WO, O_WO, x)
        for kb in range(KB):
            dve.wait_ge(S("mem_hi"), kb + 1)
            V.tensor_tensor(mem[1][:, kb], memraw[:, kb], mem[0][:, kb].bitcast(f32), sub).then_inc(S("mem_lo"), 1)
        normalise("ln1", h1)


        ch = own

        def row_max(n, bank):
            V.tensor_reduce(amax[:, n:n + 2], bank[:, :].rearrange("p (t m) -> p t m", m=N_MEM), X, ALU.max)\
                .then_inc(S("att_max"), 1)

        for h in range(X_HEADS + 1):
            if h < X_HEADS:
                dve.wait_ge(S("att_sc"), h + 1)
                if h:
                    dve.wait_ge(S("att_exp"), TILES * h)
                row_max(0, ps[0])
                row_max(2, ps[1])
                dve.wait_ge(S("att_max"), 3 * h + 2)
                V.tensor_scalar(amax, amax, -1.0, None, mul).then_inc(S("att_max"), 1)
                dve.wait_ge(S("att_exp"), TILES * (h + 1))
                ch(V.reciprocal(asum, asum))
                V.tensor_tensor(ap[:], ap[:], bc(asum, N_MEM), mul).then_inc(S("att_p"), 1)
            if h:
                for d in range(2):
                    i = 2 * (h - 1) + d
                    dve.wait_ge(S("ao_hi"), i + 1)
                    V.tensor_tensor(ao[1][:, i, PT], ps[6 + d][:, :], ao[0][:, i, PT].bitcast(f32), sub)\
                        .then_inc(S("ao_lo"), 1)
        dve.wait_ge(S("ssc_flip"), 1)
        row_max(0, ps[3])
        dve.wait_ge(S("att_max"), 3 * X_HEADS + 1)
        V.tensor_scalar(amax[:, 0:2], amax[:, 0:2], -1.0, None, mul).then_inc(S("att_max"), 1)
        dve.wait_ge(S("att_exp"), TILES * X_HEADS + 2)
        ch(V.reciprocal(asum[:, 0:2], asum[:, 0:2]))
        V.tensor_tensor(ap[:, 0:2], ap[:, 0:2], bc(asum[:, 0:2], N_MEM), mul).then_inc(S("sp_ready"), 1)
        dve.wait_ge(S("ao_hi"), KB + 1)
        V.tensor_tensor(ao[1][:, :, ST], tiled(ps[3][:, :], SAMPLE), ao[0][:, :, ST].bitcast(f32), sub)\
            .then_inc(S("ao_lo"), 1)

        residual("ln2", C_XO, O_XO, h1)
        normalise("ln2", h2, scale_after=ALPHA)

        dve.wait_ge(S("acc_ready"), KB)
        V.memset(lns[:], 0.0).then_inc(S("ln_zero"), 1)
        dve.wait_ge(*ln("ln3", "zero", 1, 1))

        def quarter(q, last=False):
            for n in range(KB):
                dve.wait_ge(taken[n % 2], q * KB + (O_FF + n) // 2 + 1)
                V.tensor_tensor(hs[:, n % 2], ht[:, n % 2], ht[:, n % 2], mul).then_inc(S("hid_sq"), 1)
                dve.wait_ge(S("hid_sq"), q * KB + n + 1)
                dve.wait_ge(S("hid_hi"), q * KB + n + 1)
                V.tensor_tensor(hid[1][:, n], hs[:, n % 2], hid[0][:, n].bitcast(f32), sub).then_inc(S("hid_lo"), 1)
            for j in range(KB):
                dve.wait_ge(gemm_done, q * (2 * KB) + C_FF + KB + j + 1)
                V.tensor_tensor(res[:, j, HALVES[0]], res[:, j, HALVES[0]], out_pair(j)[0][:, 0:HALF], add)\
                    .then_inc(S("acc"), 1)
                V.tensor_tensor(res[:, j, HALVES[1]], res[:, j, HALVES[1]], out_pair(j)[1][:, 0:HALF], add)\
                    .then_inc(taken[j % 2], 1)
                if last:
                    dve.wait_ge(S("acc"), q * KB + j + 1)
                    dve.wait_ge(taken[j % 2], q * KB + (O_FF + KB + j) // 2 + 1)
                    V.tensor_tensor(lns[:, 0], lns[:, 0], res[:, j], add).then_inc(S("ln_sum"), 1)
                    dve.wait_ge(*ln("ln3", "sq", KB, j + 1))
                    V.tensor_tensor(lns[:, 1], lns[:, 1], lnt[:, j % 2], add).then_inc(S("ln_sum"), 1)
                    dve.wait_ge(*ln("ln3", "sum", 2 * KB, 2 * (j + 1)))

        with dve.Fori(0, QUARTERS - 1) as q:
            quarter(q)
        quarter(QUARTERS - 1, True)
        normalise("ln3", None)

    block_ctx.__exit__(None, None, None)


def _blocks(v):
    return np.ascontiguousarray(v.reshape(-1, P).T)


def _rows(a):
    return np.ascontiguousarray(a.reshape(a.shape[0], -1, P).transpose(2, 1, 0))


def _chunks(w):
    return w.reshape(KB, P, -1, P).transpose(2, 1, 0, 3)


def _shape_constants():
    i = np.arange(P)
    ident = np.eye(P, dtype=np.float32)
    triu = (i[:, None] <= i[None, :]).astype(np.float32)
    j = np.arange(SAMPLE)
    triu8 = np.zeros((P, SAMPLE), np.float32)
    triu8[:SAMPLE] = (j[:, None] <= j[None, :]) & (j[:, None] // DEC_SEQ == j[None, :] // DEC_SEQ)
    same8 = np.zeros((P, DEC_BATCH), np.float32)
    same8[:SAMPLE] = j[:, None] // DEC_SEQ == np.arange(DEC_BATCH)[None, :]
    levels = np.stack([((i[:, None] // (2 * s) == i[None, :] // (2 * s)) & (i[None, :] // s % 2 == 1)
                        & (i[:, None] // s % 2 == 0)).astype(np.float32) for s in LEVELS], axis=1)
    return np.concatenate([ident, triu, triu8, same8], axis=1), np.ascontiguousarray(levels)


def kernel(**inputs):
    import concourse.bacc as _bacc
    from concourse.bass_utils import run_bass_kernel_spmd as _run

    a = {k: np.asarray(v) for k, v in inputs.items()}
    w_in = a["w_in"][0]
    cols = {}
    off = 0
    for name, width in (("glu", 1024), ("qkv", 1536), ("og", 512), ("bd", 8), ("ga", 1024), ("gb", 1024)):
        cols[name] = _chunks(w_in[:, off:off + width]) if name != "bd" else w_in[:, off:off + width]
        off += width
    out_ab = _chunks(np.concatenate([a["w_conv_out"][0], a["w_dn_out"][0]], axis=0))
    ff1, ff2 = _chunks(a["w_ff1"][0]), a["w_ff2"][0]
    order = [cols["qkv"]]
    for i in range(CT):
        order += [cols["glu"][CT + i:CT + i + 1], cols["glu"][i:i + 1]]
    order.append(cols["og"])
    for m in range(KB):
        order += [cols["ga"][m:m + 1], cols["gb"][m:m + 1], out_ab[m:m + 1]]
    order += [_chunks(a["w_o"][0]), _chunks(a["w_mem_kv"][0]), _chunks(a["w_xq"][0]), _chunks(a["w_xo"][0])]
    for q in range(QUARTERS):
        order += [ff1[KB * q:KB * (q + 1)], _chunks(ff2[D_MODEL * q:D_MODEL * (q + 1)])]
    vectors = {
        "b_glu": _blocks(a["b_glu"][0]), "b_dw": _blocks(a["b_dw"][0]), "cg": _blocks(a["ln_conv_g"][0]),
        "cb": _blocks(a["ln_conv_b"][0]), "dng": _blocks(a["dn_norm_g"][0]),
        "g1": _blocks(a["ln1_g"][0]), "b1": _blocks(a["ln1_b"][0]), "g2": _blocks(a["ln2_g"][0]),
        "b2": _blocks(a["ln2_b"][0]), "g3": _blocks(a["ln3_g"][0]), "b3": _blocks(a["ln3_b"][0]),
        "w_dw": _rows(a["w_dw"][0]).reshape(P, -1), "w_short": _rows(a["w_short"][0]).reshape(P, -1),
        "a_log": np.tile(a["a_log"], (P, 1)), "dt_bias": np.tile(a["dt_bias"], (P, 1)),
    }
    cst, levels = _shape_constants()
    mem = a["mem_prompt"][0]
    arrays = {
        "xT": _rows(np.concatenate([a["x_prompt"][0], a["x_sample"].reshape(SAMPLE, D_MODEL)], axis=0)),
        "w": np.concatenate(order, axis=0),
        "wbd": np.ascontiguousarray(cols["bd"].reshape(KB, P, 8).transpose(1, 0, 2)),
        "par": np.concatenate([vectors[n] for n, _ in WIDTHS], axis=1),
        "cst": cst, "lmask": levels,
        "qhist": np.ascontiguousarray(a["state_qkv_conv"][0].reshape(DEC_BATCH, QH, QT, P).transpose(3, 2, 0, 1)
                                      .reshape(P, QT, DEC_BATCH * QH)),
        "chist": np.ascontiguousarray(a["state_conv"][0].reshape(DEC_BATCH, CH, CT, P).transpose(3, 2, 0, 1)),
        "sdelta": np.ascontiguousarray(a["state_delta"][0].transpose(2, 1, 0, 3)),
        "memT": _rows(mem),
        "kT": np.ascontiguousarray(a["cache_mem_k"][0].reshape(DEC_BATCH, N_MEM, KB, P).transpose(0, 3, 2, 1)
                                   .reshape(DEC_BATCH, P, KB * N_MEM)),
        "v": np.ascontiguousarray(a["cache_mem_v"][0].reshape(DEC_BATCH, 2, P, D_MODEL).transpose(0, 2, 1, 3)
                                  .reshape(DEC_BATCH, P, 2 * D_MODEL)),
    }
    outputs = {
        "qlast": (P, QT, (1 + DEC_BATCH) * QH), "pconv": (P, CT, CH), "sconv": (P, CT, DEC_BATCH, CH),
        "sdelta_out": (P, HEADS, DEC_BATCH, DK), "pdelta_out": (P, HEADS, DK),
        "mk": (P, KB, N_MEM), "mv": (P, 2, D_MODEL), "yT": (P, KB, TOK),
    }
    nc = _bacc.Bacc("TRN2", target_bir_lowering=False, num_devices=1)
    f32 = mybir.dt.float32
    aps = {n: nc.dram_tensor(n, v.shape, f32, kind="ExternalInput").ap() for n, v in arrays.items()}
    aps.update({n: nc.dram_tensor(n, s, f32, kind="ExternalOutput").ap() for n, s in outputs.items()})
    build(nc, aps)
    r = _run(nc, [arrays], core_ids=[0]).results[0]

    y = r["yT"].transpose(2, 1, 0).reshape(TOK, D_MODEL)
    ql = r["qlast"].reshape(P, QT, 1 + DEC_BATCH, QH).transpose(2, 3, 1, 0).reshape(1 + DEC_BATCH, QH, 3 * HEADS * DK)
    return (y[None, :SEQ], y[SEQ:].reshape(DEC_BATCH, DEC_SEQ, D_MODEL),
            r["pconv"].transpose(2, 1, 0).reshape(1, 1, CH, CONV_CH), ql[None, :1],
            r["pdelta_out"].transpose(1, 0, 2)[None, None],
            r["mk"].transpose(2, 1, 0).reshape(1, 1, N_MEM, X_HEADS, X_DIM),
            r["mv"].transpose(1, 0, 2).reshape(1, 1, N_MEM, X_HEADS, X_DIM),
            r["sconv"].transpose(2, 3, 1, 0).reshape(1, DEC_BATCH, CH, CONV_CH), ql[None, 1:],
            r["sdelta_out"].transpose(2, 1, 0, 3)[None])
```

```python
import numpy as np

import concourse.bass as bass
from concourse import mybir
from concourse.alu_op_type import AluOpType as ALU

D_MODEL, SEQ, DEC_BATCH, DEC_SEQ, N_MEM = 1024, 512, 8, 8, 256
CONV_CH, CONV_K, SHORT_K = 512, 31, 4
HEADS, DK = 4, 128
X_HEADS, X_DIM = 4, 256
D_FF = 4 * D_MODEL
ALPHA = 2.0 ** 0.25
LN_EPS, RMS_EPS, L2_EPS = 1e-5, 1e-6, 1e-6

P = 128
SAMPLE = DEC_BATCH * DEC_SEQ
TOK = SEQ + SAMPLE
HALF = TOK // 2
KB = D_MODEL // P
RING, RAW = 4, 2
CT = CONV_CH // P
QT = 3 * HEADS
TILES = SEQ // P
CH, QH = CONV_K - 1, SHORT_K - 1
UP, US = CH + SEQ, CH + DEC_SEQ
RP, RS = QH + SEQ, QH + DEC_SEQ
QUARTERS = D_FF // D_MODEL

C_QKV, C_GLU, C_OG, C_GA, C_MIX, C_WO, C_MEM, C_XQ, C_XO, C_FF = 0, 12, 20, 24, 32, 48, 56, 72, 80, 88
CHUNKS = 152
O_QKV, O_GLU, O_OG, O_GA, O_GB, O_WO, O_MEM, O_XQ, O_XO, O_FF = 0, 12, 20, 24, 32, 40, 48, 64, 72, 80
FILL = C_MIX - C_GLU
SLICES = 4

WIDTHS = [("b_glu", 8), ("b_dw", 4), ("cg", 4), ("cb", 4), ("dng", 1), ("g1", 8), ("b1", 8), ("g2", 8), ("b2", 8),
          ("g3", 8), ("b3", 8), ("w_dw", CT * CONV_K), ("w_short", QT * SHORT_K), ("a_log", 4), ("dt_bias", 4)]
PAR = {n: sum(w for _, w in WIDTHS[:i]) for i, (n, _) in enumerate(WIDTHS)}
NPAR = sum(w for _, w in WIDTHS)
LEVELS = [1, 2, 4, 8, 16, 32, 64]


def build(nc, A):
    f32, f32r = mybir.dt.float32, mybir.dt.float32r
    ACT = mybir.ActivationFunctionType
    X = mybir.AxisListType.X
    mul, add, sub = ALU.mult, ALU.add, ALU.subtract

    BASE, KIB = 16512, 1024
    R0, R1, R2, R3 = 48, 84, 120, 156

    def at(name, kib, shape, dtype=f32):
        return nc.alloc_sbuf_tensor_at(name, shape, dtype, offset=BASE + int(kib * KIB))

    def pair(name, kib, n=KB, w=TOK):
        return (at(name + "_hi", kib, [P, n, w], f32r), at(name + "_lo", kib + n * w * 4 / KIB, [P, n, w], f32r))

    raw = at("w_raw", 0, [P, RAW, KB, P])
    whi = at("w_hi", 8, [P, RING, KB, P], f32r)
    wlo = at("w_lo", 24, [P, RING, KB, P], f32r)
    sig = at("sig", 40, [P, 2, TOK])
    pst = at("pst", 44.5, [P, HEADS, DK])
    wbd = at("wbd", 46.5, [P, KB, 8])
    bdw = pair("bdw", 46.75, KB, 8)

    x = pair("x", R0)
    kv = at("kv", R0, [P, 4, 2 * X_HEADS * N_MEM])
    h2 = pair("h2", R0)

    xraw = at("xraw", R1 + 18, [P, KB, TOK])
    u = at("u", R1, [P, CT, UP + DEC_BATCH * US])
    sga = at("sga", R1 + 18, [P, KB, TOK])
    memraw = at("memraw", R1, [P, KB, N_MEM])
    mem = pair("mem", R1 + 8, KB, N_MEM)
    ao = pair("ao", R1)

    qraw = at("qraw", R2, [P, QT, RP + DEC_BATCH * RS])
    qhist = at("qhist", R2 + 28.5, [P, QT, DEC_BATCH * QH])
    qlast = at("qlast", R2 + 30, [P, QT, (1 + DEC_BATCH) * QH])
    dl = at("dl", R2, [P, 2, 8, SEQ])
    sst = [at(f"sst{h}", R2 + (h + 1) % HEADS * 4, [P, DEC_BATCH, DK]) for h in range(HEADS)]
    sw = at("sw", R2 + 16, [P, 8, HEADS, SAMPLE])
    sktm = at("sktm", R2 + 20, [P, DEC_BATCH, DK])
    skt = at("skt", R2 + 24, [P, HEADS, DK])
    sz = at("sz", R2 + 26, [P, HEADS, DK])
    sld = at("sld", R2 + 26, [P, HEADS, DK])
    su = at("su", R2 + 28, [P, HEADS, DK])
    szt = at("szt", R2 + 30, [P, HEADS, SAMPLE])
    tmp = at("tmp", R2, [P, 2, TOK])
    nrm = at("nrm", R2 + 4.5, [P, 2, TOK])
    lmask = at("lmask", R2 + 32, [P, len(LEVELS), P])
    mixed = pair("mixed", R2)
    h1 = pair("h1", R2)
    hid = pair("hid", R2)

    qkv = at("qkv", R3, [P, QT, TOK])
    z = (at("z_hi", R1, [P, KB, TOK], f32r), at("z_lo", R3, [P, KB, TOK], f32r))
    gb = at("gb", R3 + 18, [P, 2, TOK])
    mx = at("mx", R3 + 22.5, [P, 2, 2, TOK])
    res = at("res", R3, [P, KB, TOK])
    aq = at("aq", R3, [P, KB, TOK])
    mk = at("mk", R3 + 18, [P, KB, N_MEM])
    mv = at("mv", R3 + 26, [P, 2, D_MODEL])
    ht = at("ht", R3 + 18, [P, 2, TOK])
    hs = at("hs", R3 + 22.5, [P, 2, TOK])
    sgate = at("sgate", R3 + 27, [P, HEADS, TOK])
    cv = at("cv", R3 + 36, [P, CT, TOK])
    l2s, l2r = cv[:, 2:4], sgate[:, 0:2]
    bdr = at("bdr", R3 + 36, [8, TOK])
    lns = at("lns", R3 + 34, [P, 2, TOK])
    lnt = at("lnt", R3 + 38.5, [P, 2, TOK])
    ap = at("att_p", R3 + 34, [P, 4, N_MEM])
    apt = at("att_pt", R3 + 38, [P, 2, SEQ])
    aps = at("att_ps", 40, [P, 2, N_MEM])
    ssc = at("att_s", R3 + 42, [P, 2, 2 * P])
    cst = at("cst", R3 + 45, [P, 328])
    ident, triu, triu8, same8 = cst[:, 0:128], cst[:, 128:256], cst[:, 256:320], cst[:, 320:328]
    ones = at("ones", R3 + 46.5, [P, 4, P])
    par = at("par", R3 + 48.5, [P, NPAR])
    sm = at("sm", R3 + 49.75, [P, 260])
    eps_ln, eps_l2, eps_rows = sm[:, 256:257], sm[:, 257:258], sm[0:8, 258:259]
    row_of = at("row_of", R3 + 50.8125, [P, 3, 16])
    assert RMS_EPS == L2_EPS

    def cols(a, n, c):
        return sm[:, a:a + n * c].rearrange("p (t c) -> p t c", c=c)

    bd, beta, ld, gcol, sp0, sp1 = cols(0, 5, 8), cols(40, 5, 4), cols(60, 5, 4), cols(80, 5, 4), cols(100, 5, 4), \
        cols(120, 5, 4)
    nega, etail, eglast, seglast, stail = sm[:, 140:144], cols(144, 2, 4), cols(152, 2, 4), cols(160, 4, 8), \
        sm[:, 192:196]
    amax, asum = sm[:, 200:204], sm[:, 208:212]
    samax, sasum = sm[:, 216:218], sm[:, 218:220]

    ps = [nc.alloc_psum_tensor(f"bank{i}", [P, 512], f32) for i in range(8)]
    HALVES = (slice(0, HALF), slice(HALF, TOK))
    PT, ST, SL = slice(0, SEQ), slice(SEQ, TOK), slice(0, SAMPLE)

    def out_pair(o):
        return ps[2 * (o % 2)], ps[2 * (o % 2) + 1]

    def pc(name, i=0):
        return par[:, PAR[name] + i:PAR[name] + i + 1]

    def bc(a, n):
        return a.unsqueeze(2).broadcast_to([a.shape[0], a.shape[1], n])

    def rep(a, n):
        return a.unsqueeze(1).broadcast_to([a.shape[0], n, a.shape[1]])

    def tiled(a, n=P):
        return a.rearrange("p (c i) -> p c i", i=n)

    def u_s(j):
        return u[:, j, UP:].rearrange("p (b t) -> p b t", t=US)

    K_, V_, NB_, QK_, X_, Y_, P_, W_ = range(8)
    S_NB, S_QK, S_X, S_Y, S_P, S_W, S_D, S_E = range(8)

    def dt(hh, k):
        return tiled(dl[:, hh, k])

    sems = {}

    def S(name):
        if name not in sems:
            sems[name] = nc.alloc_semaphore(name)
        return sems[name]

    raw_loaded = [S(f"raw_loaded{i}") for i in range(RAW)]
    hi_ready, lo_ready, gemm_done = S("hi_ready"), S("lo_ready"), S("gemm_done")
    taken = [S("taken0"), S("taken1")]
    stored = S("stored")
    N_STORES = 1 + 1 + 2 * CT + 2 + KB
    CONSTS = 13

    def at_head(pr, hh):
        return 2 * pr + hh + 1

    def at_level(pr, n, hh):
        return (pr * len(LEVELS) + n) * 2 + hh + 1

    def at_tile(pr, c, hh):
        return (pr * TILES + c) * 2 + hh + 1

    def ln(name, what, steps, n):
        return S("ln_" + what), (int(name[2]) - 1) * steps + n

    class Chain:

        def __init__(self, eng, name, start=0):
            self.eng, self.sem, self.n, self.start = eng, S(name), 0, start

        def step(self, ins):
            self.n += 1
            ins.then_inc(self.sem, 1)

        def wait(self, back=0):
            if self.n > back:
                self.eng.wait_ge(self.sem, self.start + self.n - back)

        def __call__(self, ins):
            self.step(ins)
            self.wait()

    block_ctx = nc.Block()
    block = block_ctx.__enter__()

    @block.sync
    def _(sp):
        def load_x(i):
            sp.dma_start(xraw[:, 2 * i:2 * i + 2], A["xT"][:, 2 * i:2 * i + 2]).then_inc(S(f"x_loaded{i}"), 16)

        def load_w(c):
            if c >= RAW:
                sp.wait_ge(lo_ready, c - RAW + 1)
            sp.dma_start(raw[:, c % RAW], A["w"][c]).then_inc(raw_loaded[c % RAW], 16)

        load_x(0)
        load_w(0)
        for i in range(1, 4):
            load_x(i)
        load_w(1)
        sp.dma_start(wbd[:], A["wbd"][:]).then_inc(S("par_loaded"), 16)
        sp.dma_start(par[:], A["par"][:]).then_inc(S("par_loaded"), 16)
        sp.dma_start(qhist[:], A["qhist"][:]).then_inc(S("par_loaded"), 16)
        load_w(2)
        load_w(3)
        sp.dma_start(cst[:], A["cst"][:]).then_inc(S("cst_loaded"), 16)
        sp.dma_start(lmask[:], A["lmask"][:]).then_inc(S("cst_loaded"), 16)
        for j in range(CT):
            sp.dma_start(u_s(j)[:, :, 0:CH], A["chist"][:, j]).then_inc(S("cst_loaded"), 16)

        def weights(first, last):
            with sp.Fori(0, (last - first) // RING) as g:
                for s in range(RING):
                    chunk = sp.snap(g * RING + first + s)
                    used = sp.snap(g * RING + first + s - RAW + 1)
                    sp.wait_ge(lo_ready, used)
                    sp.dma_start(raw[:, s % RAW], A["w"][chunk]).then_inc(raw_loaded[s % RAW], 16)

        weights(4, C_GLU + 8)
        sp.wait_ge(S("qraw_free"), 1)
        for h in range(HEADS):
            sp.dma_start(sst[h][:], A["sdelta"][:, h]).then_inc(S("sst_loaded"), 16)
        weights(C_GLU + 8, C_WO + 4)
        sp.wait_ge(gemm_done, C_WO)
        sp.dma_start(memraw[:], A["memT"][:]).then_inc(S("mem_loaded"), 16)
        weights(C_WO + 4, C_XQ + 4)
        sp.wait_ge(*ln("ln1", "res", KB, KB))
        for i in range(2 * DEC_BATCH):
            if i >= 4:
                sp.wait_ge(S("kv_used"), i - 3)
            sp.dma_start(kv[:, i % 4], (A["kT"] if i < DEC_BATCH else A["v"])[i % DEC_BATCH])\
              .then_inc(S(f"kv_loaded{i % 4}"), 16)
            if i == 3:
                weights(C_XQ + 4, C_XO + 4)
        weights(C_XO + 4, CHUNKS)
        sp.wait_ge(stored, 16 * N_STORES)
        sp.wait_ge(S("states_out"), 16 * (HEADS - 1))
        sp.wait_ge(S("last_state_out"), 16)

    @block.gpsimd
    def _(pool):
        for i, v in enumerate((1.0, 1 / 128, 1 / 512, 1 / 1024)):
            nc.gpsimd.memset(ones[:, i], v).then_inc(S("consts"), 1)
        nc.gpsimd.memset(eps_ln, LN_EPS).then_inc(S("consts"), 1)
        nc.gpsimd.memset(eps_l2, L2_EPS).then_inc(S("consts"), 1)
        nc.gpsimd.memset(u[:, :, 0:CH], 0.0).then_inc(S("consts"), 1)
        nc.gpsimd.memset(row_of[:], 0.0).then_inc(S("consts"), 1)
        nc.gpsimd.memset(eps_rows, RMS_EPS).then_inc(S("consts"), 1)
        pool.wait_ge(S("consts"), 9)
        for i, v in enumerate((1.0, 1 / 512, 1 / 128)):
            nc.gpsimd.memset(row_of[:, i, 8:9], v).then_inc(S("consts"), 1)
        nc.gpsimd.memset(eps_rows[0:1], LN_EPS).then_inc(S("consts"), 1)

        def lo_parts(first, last):
            with pool.Fori(first // RING, last // RING) as g:
                for s in range(RING):
                    pool.wait_ge(hi_ready, g * RING + s + 1)
                    nc.gpsimd.tensor_tensor(wlo[:, s], raw[:, s % RAW], whi[:, s].bitcast(f32), sub)\
                        .then_inc(lo_ready, 1)

        lo_parts(0, C_FF + RING)
        for j in range(KB):
            pool.wait_ge(*ln("ln2", "hi", KB, j + 1))
            nc.gpsimd.tensor_tensor(h2[1][:, j], res[:, j], h2[0][:, j].bitcast(f32), sub).then_inc(S("ln_out"), 1)
        lo_parts(C_FF + RING, CHUNKS)

    @block.tensor
    def _(pe):
        SPANS = ((0, HALF), (HALF, TOK))
        every = [(kb, None) for kb in range(KB)]

        def gemm(slot, out, xs, kbs, spans=SPANS, opens=True, closes=True):
            for i, (kb, ready) in enumerate(kbs):
                if ready is not None:
                    pe.wait_ge(*ready)
                for bank, (a, b) in zip(out, spans):
                    for j, (w, m) in enumerate(((whi, xs[0]), (whi, xs[1]), (wlo, xs[0]))):
                        ins = nc.tensor.matmul(bank[:, 0:b - a], lhsT=w[:, slot, kb], rhs=m[:, kb, a:b],
                                               start=(opens and i == 0 and j == 0),
                                               stop=(closes and i == len(kbs) - 1 and j == 2))
            return ins

        def phase(c0, o0, n, xs, kbs, spans=SPANS):
            def group(g, fresh=False):
                for s in range(RING):
                    pe.wait_ge(lo_ready, g * RING + c0 + s + 1)
                    if not (fresh and s < 2):
                        pe.wait_ge(taken[s % 2], g * 2 + (o0 + s) // 2)
                    gemm(s, out_pair(o0 + s), xs, kbs, spans).then_inc(gemm_done, 1)
            if o0 == 0:
                group(0, True)
                beta_decay()
            first = 1 if o0 == 0 else 0
            if n // RING - first == 1:
                return group(first)
            with pe.Fori(first, n // RING) as g:
                group(g)

        def ln_average(name):
            pe.wait_ge(*ln(name, "sum", 2 * KB, 2 * KB))
            for i in range(2):
                for h, half in enumerate(HALVES):
                    ins = nc.tensor.matmul(ps[4 + 2 * i + h][:, 0:HALF], lhsT=ones[:, 3], rhs=lns[:, i, half],
                                           start=True, stop=True)
            ins.then_inc(S("ln_avg"), 1)

        def beta_decay():
            pe.wait_ge(S("bdw_split"), 2)
            for kb in range(KB):
                for h, half in enumerate(HALVES):
                    for j, (w, m) in enumerate(((bdw[0], x[0]), (bdw[0], x[1]), (bdw[1], x[0]))):
                        ins = nc.tensor.matmul(ps[4 + h][0:8, 0:HALF], lhsT=w[:, kb], rhs=m[:, kb, half],
                                               start=(kb == 0 and j == 0), stop=(kb == KB - 1 and j == 2))
            ins.then_inc(S("bd_done"), 1)

        phase(C_QKV, O_QKV, 12, x, [(kb, (S("x_lo"), kb + 1)) for kb in range(KB)])

        def filler():
            for f in range(FILL):
                c, o = C_GLU + f, O_GLU + f
                pe.wait_ge(lo_ready, c + 1)
                pe.wait_ge(taken[o % 2], o // 2)
                for n in range(SLICES):
                    ins = gemm(c % RING, out_pair(o), x, every[2 * n:2 * n + 2], opens=(n == 0), closes=(n == SLICES - 1))
                    if n == SLICES - 1:
                        ins.then_inc(gemm_done, 1)
                    yield

        fill = filler()

        def between(n=1):
            for _ in range(n):
                next(fill, None)

        T = nc.tensor
        between(SLICES)
        pe.wait_ge(S("cst_loaded"), 16 * (2 + CT))
        pe.wait_ge(S("bd_rows"), 2)
        for t in range(5):
            n = P if t < TILES else SAMPLE
            ins = T.transpose(ps[6][0:n, 8 * t:8 * t + 8], bdr[:, t * P:t * P + n], ident[0:8, 0:8])
        ins.then_inc(S("bd_flip"), 1)

        def sum_rows(out, which, i, src, start, stop):
            for h, half in enumerate(HALVES):
                ins = T.matmul(out[h][0:8, 0:HALF], lhsT=row_of[:, which, 8 - i:16 - i], rhs=src[:, half],
                               start=start, stop=stop)
            return ins

        def spread(out, i, src):
            for h, half in enumerate(HALVES):
                ins = T.matmul(out[h][:, 0:HALF], lhsT=ident[0:8, i:i + 1].broadcast_to([8, P]), rhs=src[0:8, half],
                               start=True, stop=True)
            return ins

        pe.wait_ge(S("consts"), CONSTS)
        for i in range(2 * HEADS):
            pe.wait_ge(S("l2_sq"), i + 1)
            sum_rows((ps[4], ps[5]), 0, i, l2s[:, i % 2], i == 0, i == 2 * HEADS - 1).then_inc(S("l2_sum"), 1)
        between(2)
        pe.wait_ge(S("ld_ready"), 1)
        nc.tensor.matmul(ps[7][:, 64:64 + 16], lhsT=triu, rhs=ld[:, 0:TILES], start=True, stop=True)
        nc.tensor.matmul(ps[7][SL, 80:84], lhsT=triu8[SL], rhs=ld[SL, TILES], start=True, stop=True)\
            .then_inc(S("g_done"), 1)
        between(2)
        pe.wait_ge(S("l2_inv"), 1)
        pe.wait_ge(S("gcol_ready"), 1)
        for i in range(2 * HEADS):
            if i >= 2:
                pe.wait_ge(S("l2_done"), i - 1)
            spread((ps[6], ps[7]) if i % 2 == 0 else (ps[4], ps[5]), i, l2r[:, 0]).then_inc(S("l2_bc"), 1)

        pe.wait_ge(S("sld_ready"), 1)
        for h in range(HEADS):
            ins = T.matmul(ps[4][:, h * SAMPLE:(h + 1) * SAMPLE], lhsT=sld[SL, h], rhs=triu8[SL], start=True, stop=True)
        ins.then_inc(S("s_grow"), 1)
        for h in range(HEADS):
            k, q = qkv[:, HEADS + h, ST], qkv[:, h, ST]
            T.matmul(ps[5][SL, h * SAMPLE:(h + 1) * SAMPLE], lhsT=k, rhs=k, start=True, stop=True)
            ins = T.matmul(ps[5][SL, (4 + h) * SAMPLE:(5 + h) * SAMPLE], lhsT=k, rhs=q, start=True, stop=True)
        ins.then_inc(S("s_kk"), 1)
        for h in range(HEADS):
            ins = T.transpose(ps[6][SL, h * DK:(h + 1) * DK], qkv[:, HEADS + h, ST], ident)
        ins.then_inc(S("s_kt"), 1)
        between(4)

        def sw_all(bank, a, b, width=SAMPLE, off=0):
            for h in range(HEADS):
                ins = T.matmul(bank[SL, off + h * width:off + (h + 1) * width], lhsT=a(h), rhs=b(h), start=True,
                               stop=True)
            return ins

        for n in range(3):
            pe.wait_ge(S("s_as"), n + 1)
            if n > 0:
                pe.wait_ge(S("s_xy"), 2 * n)
            sw_all(ps[4], lambda h: sw[SL, S_W, h], lambda h: sw[SL, S_X, h] if n else ident[SL, SL])\
                .then_inc(S("s_ax"), 1)
            between()
            if n > 0:
                pe.wait_ge(S("s_p"), n)
                sw_all(ps[5], lambda h: sw[SL, S_Y, h], lambda h: sw[SL, S_P, h])
                sw_all(ps[5], lambda h: sw[SL, S_P, h], lambda h: sw[SL, S_Y, h], off=256).then_inc(S("s_xax"), 1)
                between()
        pe.wait_ge(S("sst_loaded"), 16 * HEADS)
        pe.wait_ge(S("s_scaled"), 2)
        for h in range(HEADS):
            for b in range(DEC_BATCH):
                ins = T.matmul(ps[6][:, h * SAMPLE + 8 * b:h * SAMPLE + 8 * b + 8], lhsT=sst[h][:, b],
                               rhs=qkv[:, HEADS + h, SEQ + 8 * b:SEQ + 8 * b + 8], start=True, stop=True)
        ins.then_inc(S("s_ks"), 1)
        between()
        pe.wait_ge(S("s_zt"), 1)
        for h in range(HEADS):
            ins = T.transpose(ps[7][SL, h * DK:(h + 1) * DK], szt[:, h], ident)
        ins.then_inc(S("s_ztt"), 1)
        between()
        pe.wait_ge(S("s_z"), 1)
        pe.wait_ge(S("s_xy"), 6)
        sw_all(ps[4], lambda h: sw[SL, S_Y, h], lambda h: sz[SL, h], width=DK).then_inc(S("s_yz"), 1)
        between()
        pe.wait_ge(S("s_u"), 1)
        for h in range(HEADS):
            T.matmul(ps[5][:, h * SAMPLE:(h + 1) * SAMPLE], lhsT=su[SL, h], rhs=sw[SL, S_QK, h], start=True, stop=False,
                     skip_group_check=True)
            for b in range(DEC_BATCH):
                ins = T.matmul(ps[5][:, h * SAMPLE + 8 * b:h * SAMPLE + 8 * b + 8], lhsT=sst[h][:, b],
                               rhs=qkv[:, h, SEQ + 8 * b:SEQ + 8 * b + 8], start=False, stop=(b == DEC_BATCH - 1),
                               skip_group_check=True)
        ins.then_inc(S("s_o"), 1)
        between()
        for h in range(HEADS):
            pe.wait_ge(S("s_ktm"), h + 1)
            if h > 0:
                pe.wait_ge(S("s_new"), 3 * h)
            else:
                pe.wait_ge(S("s_z"), 1)
            for b in range(DEC_BATCH):
                ins = T.matmul(ps[6 + b // 4][:, (b % 4) * DK:(b % 4 + 1) * DK], lhsT=sktm[SL, b],
                               rhs=su[SL, h], start=True, stop=True)
            ins.then_inc(S("s_ds"), 1)
            between()

        pe.wait_ge(S("s_new"), 3 * HEADS)
        pe.wait_ge(S("s_otaken"), 1)
        for pr in range(2):
            HH = range(2)
            q = [tiled(qkv[:, 2 * pr + hh, PT]) for hh in HH]
            k = [tiled(qkv[:, HEADS + 2 * pr + hh, PT]) for hh in HH]
            v = [tiled(qkv[:, 2 * HEADS + 2 * pr + hh, PT]) for hh in HH]
            b0, b1 = (ps[4], ps[6]), (ps[5], ps[7])

            def four(bank, a, b, tr=False):
                for c in range(TILES):
                    o = bank[:, c * P:(c + 1) * P]
                    ins = T.transpose(o, a(c), ident) if tr else T.matmul(o, lhsT=a(c), rhs=b(c), start=True, stop=True)
                return ins

            for hh in HH:
                pe.wait_ge(S("ldb"), at_head(pr, hh))
                if pr:
                    pe.wait_ge(S("s_new_p"), at_tile(0, TILES - 1, hh))
                    pe.wait_ge(S("o_taken"), at_tile(0, TILES - 1, hh))
                four(b0[hh], lambda c: dt(hh, X_)[:, c], lambda c: triu).then_inc(S("grow"), 1)
                four(b1[hh], lambda c: k[hh][:, c], lambda c: k[hh][:, c]).then_inc(S("kk"), 1)
            between(2)
            for hh in HH:
                pe.wait_ge(S("egrow"), at_head(pr, hh))
                four(b0[hh], lambda c: k[hh][:, c], lambda c: q[hh][:, c]).then_inc(S("qk"), 1)
                pe.wait_ge(S("nb_raw"), at_head(pr, hh))
                four(b1[hh], lambda c: k[hh][:, c], None, tr=True).then_inc(S("kt"), 1)
            between()
            for hh in HH:
                pe.wait_ge(S("qk_taken"), at_head(pr, hh))
                four(b0[hh], lambda c: v[hh][:, c], None, tr=True).then_inc(S("vt"), 1)
            between()
            for n in range(len(LEVELS)):
                for hh in HH:
                    pe.wait_ge(S("as_ready"), at_level(pr, n, hh))
                    if n == 0:
                        pe.wait_ge(S("vt_taken"), at_head(pr, hh))
                    else:
                        pe.wait_ge(S("xy"), 2 * at_level(pr, n - 1, hh) - (1 if n > 1 else 0))
                    four(b0[hh], lambda c: dt(hh, W_)[:, c], lambda c: dt(hh, X_)[:, c] if n else ident)\
                        .then_inc(S("ax"), 1)
                between()
                if n == 0:
                    continue
                for hh in HH:
                    pe.wait_ge(S("p_ready"), (pr * 6 + n - 1) * 2 + hh + 1)
                    pe.wait_ge(S("xy"), 2 * at_level(pr, n - 1, hh))
                    if n < len(LEVELS) - 1:
                        four(b1[hh], lambda c: dt(hh, Y_)[:, c], lambda c: dt(hh, P_)[:, c]).then_inc(S("xax"), 1)
                    four(b0[hh], lambda c: dt(hh, P_)[:, c], lambda c: dt(hh, Y_)[:, c]).then_inc(S("yay"), 1)
                between()
            for c in range(TILES):
                for hh in HH:
                    pe.wait_ge(S("s_new_p" if c else "scaled"), at_tile(pr, c - 1, hh) if c else 2 * at_head(pr, hh))
                    if c == 0:
                        pe.wait_ge(S("xy"), 2 * at_level(pr, len(LEVELS) - 1, hh))
                        pe.wait_ge(S("pst_zero"), 1)
                    else:
                        pe.wait_ge(S("o_taken"), at_tile(pr, c - 1, hh))
                    T.matmul(b0[hh][:, 0:DK], lhsT=k[hh][:, c], rhs=pst[:, 2 * pr + hh], start=True, stop=True)\
                        .then_inc(S("ks"), 1)
                between()
                for hh in HH:
                    pe.wait_ge(S("z_ready"), at_tile(pr, c, hh))
                    T.matmul(b1[hh][:, 0:DK], lhsT=dt(hh, Y_)[:, c], rhs=dt(hh, P_)[:, c], start=True, stop=True)\
                        .then_inc(S("yz"), 1)
                between()
                for hh in HH:
                    pe.wait_ge(S("u_ready"), at_tile(pr, c, hh))
                    T.matmul(b1[hh][:, 0:DK], lhsT=dt(hh, K_)[:, c], rhs=dt(hh, W_)[:, c], start=True, stop=True)\
                        .then_inc(S("ku"), 1)
                    T.matmul(b0[hh][:, 0:P], lhsT=pst[:, 2 * pr + hh], rhs=q[hh][:, c], start=True, stop=False)
                    T.matmul(b0[hh][:, 0:P], lhsT=dt(hh, W_)[:, c], rhs=dt(hh, QK_)[:, c], start=False, stop=True)\
                        .then_inc(S("o_done"), 1)
                between()
        between(FILL * SLICES)

        pe.wait_ge(S("o_taken"), at_tile(1, TILES - 1, 1))
        for j in range(CT):
            pe.wait_ge(S("cv_sq"), j + 1)
            sum_rows((ps[4], ps[5]), 1, 0, cv[:, j], j == 0, j == CT - 1)
            sum_rows((ps[6], ps[7]), 1, 0, tmp[:, j % 2], j == 0, False).then_inc(S("cv_avg"), 1)
        for h in range(HEADS):
            pe.wait_ge(S("rms_sq"), h + 1)
            sum_rows((ps[6], ps[7]), 2, 1 + h, sig[:, h % 2], False, h == HEADS - 1).then_inc(S("rms_avg"), 1)

        def gate_b(c, m, again=0):
            pe.wait_ge(lo_ready, again * RING + c + 1)
            pe.wait_ge(taken[m % 2], again + (O_GB + m) // 2)
            gemm(c % RING, out_pair(m), x, every).then_inc(gemm_done, 1)

        def branches(c, m, again=0):
            pe.wait_ge(lo_ready, again * RING + c + 1)
            pe.wait_ge(S("mix_free"), again * 2 + m + 1)
            gemm(c % RING, (ps[4], ps[5]), z, z_ready[0:CT])
            gemm(c % RING, (ps[6], ps[7]), z, z_ready[CT:KB]).then_inc(gemm_done, 1)

        z_ready = [(kb, (S("z_lo"), kb + 1)) for kb in range(KB)]
        gate_b(C_MIX, 0)
        pe.wait_ge(S("n_inv"), 1)
        spread((ps[4], ps[5]), 0, nrm[:, 0])
        spread((ps[6], ps[7]), 0, nrm[:, 1]).then_inc(S("n_bc"), 1)
        gate_b(C_MIX + 1, 1)
        for h in range(HEADS):
            pe.wait_ge(*((S("cv_norm"), CT) if h < 2 else (S("rms_out"), h - 1)))
            spread((ps[4], ps[5]) if h % 2 == 0 else (ps[6], ps[7]), 1 + h, nrm[:, 1]).then_inc(S("n_bc"), 1)
        with pe.Fori(0, 3) as it:
            for n in range(2):
                branches(C_MIX + 2 + 2 * n, n, it)
                gate_b(C_MIX + 3 + 2 * n, n + 2, it)
        branches(C_MIX + 14, 6)
        branches(C_MIX + 15, 7)

        phase(C_WO, O_WO, 8, mixed, [(kb, (S("mixed_lo"), kb + 1)) for kb in range(KB)])
        mem_kbs = [(kb, (S("mem_lo"), kb + 1)) for kb in range(KB)]
        phase(C_MEM, O_MEM, 4, mem, mem_kbs, ((0, N_MEM),))
        ln_average("ln1")
        phase(C_MEM + 4, O_MEM + 4, 4, mem, mem_kbs, ((0, N_MEM),))
        with pe.Fori(0, 2) as g:
            for s in range(0, RING, 2):
                o = O_MEM + 8 + s
                pe.wait_ge(lo_ready, g * RING + C_MEM + 8 + s + 2)
                for mb in range(2):
                    pe.wait_ge(taken[mb], g * 2 + (o + mb) // 2)
                    for kb in range(KB):
                        for j, (a, w) in enumerate(((mem[0], whi), (mem[1], whi), (mem[0], wlo))):
                            ins = nc.tensor.matmul(out_pair(mb)[0][:, 0:2 * P], lhsT=a[:, kb, mb * P:mb * P + P],
                                                   rhs=w[:, s:s + 2, kb], start=(kb == 0 and j == 0),
                                                   stop=(kb == KB - 1 and j == 2))
                ins.then_inc(gemm_done, 2)
        phase(C_XQ, O_XQ, 8, h1, [(kb, ln("ln1", "out", KB, kb + 1)) for kb in range(KB)])

        pe.wait_ge(taken[0], O_XO // 2)
        pe.wait_ge(taken[1], O_XO // 2)

        def scores(h):
            if h:
                pe.wait_ge(S("att_exp"), 4 * h)
            for t in range(TILES):
                for d in range(2):
                    ins = T.matmul(ps[t // 2][:, (t % 2) * N_MEM:(t % 2 + 1) * N_MEM],
                                   lhsT=aq[:, 2 * h + d, t * P:(t + 1) * P], rhs=mk[:, 2 * h + d],
                                   start=(d == 0), stop=(d == 1))
            ins.then_inc(S("att_sc"), 1)

        def flip(h):
            pe.wait_ge(S("att_p"), h + 1)
            if h:
                pe.wait_ge(S("att_pt"), 2 * h)
            for mb in range(2):
                for t in range(TILES):
                    ins = T.transpose(ps[4 + mb][:, t * P:(t + 1) * P], ap[:, t, mb * P:(mb + 1) * P], ident)
            ins.then_inc(S("att_flip"), 1)

        def values(h):
            pe.wait_ge(S("att_pt"), 2 * (h + 1))
            if h:
                pe.wait_ge(S("ao_lo"), 2 * h)
            for d in range(2):
                for mb in range(2):
                    ins = T.matmul(ps[6 + d][:, :], lhsT=mv[:, mb, (2 * h + d) * P:(2 * h + d + 1) * P],
                                   rhs=apt[:, mb], start=(mb == 0), stop=(mb == 1))
            ins.then_inc(S("att_o"), 1)

        def sample_scores(b):
            pe.wait_ge(S(f"kv_loaded{b % 4}"), 16 * (b // 4 + 1))
            for h in range(X_HEADS):
                for mb in range(2):
                    for d in range(2):
                        a = (2 * h + d) * N_MEM + mb * P
                        col = mb * N_MEM + (b * X_HEADS + h) * DEC_SEQ
                        ins = T.matmul(ps[2][:, col:col + DEC_SEQ], lhsT=kv[:, b % 4, a:a + P],
                                       rhs=aq[:, 2 * h + d, SEQ + 8 * b:SEQ + 8 * b + 8], start=(d == 0), stop=(d == 1))
            ins.then_inc(S("kv_used"), 1)

        scores(0)
        for h in range(2):
            for b in range(4):
                sample_scores(4 * h + b)
            flip(h)
            scores(h + 1)
            values(h)
        pe.wait_ge(S("ssc_ready"), 1)
        for g in range(2):
            for mb in range(2):
                ins = T.transpose(ps[3][:, g * N_MEM + mb * P:g * N_MEM + (mb + 1) * P], ssc[:, mb, g * P:(g + 1) * P],
                                  ident)
        ins.then_inc(S("ssc_flip"), 1)

        def flip_samples():
            pe.wait_ge(S("sp_ready"), 1)
            for mb in range(2):
                for g in range(2):
                    ins = T.transpose(ps[2][:, mb * N_MEM + g * P:mb * N_MEM + (g + 1) * P],
                                      aps[:, g, mb * P:(mb + 1) * P], ident)
            ins.then_inc(S("sp_flip"), 1)

        def sample_values(b):
            i = DEC_BATCH + b
            pe.wait_ge(S(f"kv_loaded{i % 4}"), 16 * (i // 4 + 1))
            for hd in range(2 * X_HEADS):
                for mb in range(2):
                    col = (b * X_HEADS + hd // 2) * DEC_SEQ
                    ins = T.matmul(ps[3][:, hd * SAMPLE + 8 * b:hd * SAMPLE + 8 * b + 8],
                                   lhsT=kv[:, i % 4, mb * D_MODEL + hd * P:mb * D_MODEL + (hd + 1) * P],
                                   rhs=ssc[:, mb, col:col + DEC_SEQ], start=(mb == 0), stop=(mb == 1))
            ins.then_inc(S("kv_used"), 1)

        flip(2)
        scores(3)
        flip_samples()
        values(2)
        pe.wait_ge(S("spt_ready"), 1)
        for b in range(4):
            sample_values(b)
        flip(3)
        for b in range(4, DEC_BATCH):
            sample_values(b)
        values(3)

        pe.wait_ge(S("ao_lo"), KB + 1)
        phase(C_XO, O_XO, 8, ao, every)
        ln_average("ln2")
        with pe.Fori(0, QUARTERS) as q:
            for n in range(2 * KB):
                xs = h2 if n < KB else hid
                pe.wait_ge(lo_ready, q * 2 * KB + C_FF + n + 1)
                pe.wait_ge(taken[n % 2], q * KB + (O_FF + n) // 2)
                if n == 0:
                    kbs = [(kb, ln("ln2", "out", KB, kb + 1)) for kb in range(KB)]
                elif n == KB:
                    kbs = [(kb, (S("hid_lo"), q * KB + kb + 1)) for kb in range(KB)]
                else:
                    kbs = every
                gemm(n % RING, out_pair(n), xs, kbs).then_inc(gemm_done, 1)
        ln_average("ln3")

    @block.scalar
    def _(act):
        A_ = nc.scalar.activation

        def split(c, turns=0):
            act.wait_ge(raw_loaded[c % RAW], turns * 16 + 16 * (c // RAW + 1))
            A_(whi[:, c % RING], raw[:, c % RAW], ACT.Copy).then_inc(hi_ready, 1)

        def store(dst, src):
            act.dma_start(dst, src).then_inc(stored, 16)

        for kb in range(KB):
            if kb % 2 == 0:
                act.wait_ge(S(f"x_loaded{kb // 2}"), 16)
            A_(x[0][:, kb], xraw[:, kb], ACT.Copy).then_inc(S("x_hi"), 1)
            if kb == 1:
                split(0)
        for c in range(1, RING):
            split(c)
        act.wait_ge(S("par_loaded"), 48)
        A_(bdw[0][:], wbd[:], ACT.Copy).then_inc(S("bdw_split"), 1)

        act.wait_ge(S("q_pad"), 2)
        with act.Fori(0, QT // RING) as g:
            for s in range(RING):
                j = act.snap(g * RING + s)
                lo, hi = out_pair(s)
                act.wait_ge(gemm_done, g * RING + s + 1)
                A_(qraw[:, bass.ds(j, 1), QH:QH + HALF], lo[:, 0:HALF].unsqueeze(1), ACT.Copy)
                A_(qraw[:, bass.ds(j, 1), QH + HALF:RP], hi[:, 0:SEQ - HALF].unsqueeze(1), ACT.Copy)
                A_(qraw[:, bass.ds(j, 1), RP:].rearrange("p o (b t) -> p (o b) t", t=RS)[:, :, QH:],
                   tiled(hi[:, SEQ - HALF:HALF], DEC_SEQ), ACT.Copy).then_inc(taken[s % 2], 1)
                split(RING + s, 2 * g)
                act.wait_ge(S("q_conv"), g * (8 * RING) + 8 * (s + 1))
                A_(sig[:, s % 2], qkv[:, bass.ds(j, 1)].rearrange("p o t -> p (o t)"), ACT.Sigmoid)\
                    .then_inc(S("q_sig"), 1)

        def filler():
            for f in range(FILL):
                c, o = C_GLU + f, O_GLU + f
                for _ in range(SLICES - 1):
                    yield
                act.wait_ge(gemm_done, c + 1)
                dst = None
                if c < C_OG:
                    i = f // 2
                    if f % 2 == 0:
                        if i < 2:
                            act.wait_ge(S("q_silu"), QT - 1 + i)
                        else:
                            act.wait_ge(taken[1], O_GLU // 2 + i - 1)
                        dst, bias, signal = sig[:, i % 2], pc("b_glu", CT + i), taken[0]
                elif c < C_GA:
                    i = c - C_OG
                    if i < 2:
                        act.wait_ge(taken[1], O_GLU // 2 + i + 3)
                    else:
                        act.wait_ge(taken[o % 2], o // 2)
                    dst, bias, signal = sig[:, i % 2], 0.0, S("og_sig")
                else:
                    dst, bias, signal = sga[:, c - C_GA], 0.0, taken[o % 2]
                if dst is not None:
                    for h, half in enumerate(HALVES):
                        ins = A_(dst[:, half], out_pair(o)[h][:, 0:HALF], ACT.Sigmoid, bias=bias)
                    ins.then_inc(signal, 1)
                split(c + RING)
                yield

        fill = filler()

        def between(n=1):
            for _ in range(n):
                next(fill, None)

        act.wait_ge(S("bd_done"), 1)
        for h, half in enumerate(HALVES):
            A_(bdr[:, half], ps[4 + h][0:8, 0:HALF], ACT.Copy).then_inc(S("bd_rows"), 1)
        act.wait_ge(S("consts"), CONSTS)
        act.wait_ge(S("q_silu"), 2 * HEADS)
        for i in range(2 * HEADS):
            if i >= 2:
                act.wait_ge(S("l2_sum"), i - 1)
            A_(l2s[:, i % 2], qkv[:, i], ACT.Square).then_inc(S("l2_sq"), 1)
        act.wait_ge(S("l2_sum"), 2 * HEADS)
        for h, half in enumerate(HALVES):
            A_(l2r[0:8, 0, half], ps[4 + h][0:8, 0:HALF], ACT.Sqrt, bias=eps_l2[0:8]).then_inc(S("l2_root"), 1)
        between(2)
        act.wait_ge(S("dve_own"), 5)
        A_(beta, bd[:, :, 0:4], ACT.Sigmoid).then_inc(S("beta_ready"), 1)
        ch = Chain(act, "act_ld")
        ch(A_(sp1, sp1, ACT.Exp))
        A_(nega, par[:, PAR["a_log"]:PAR["a_log"] + 4], ACT.Exp).then_inc(S("exp_ready"), 1)
        act.wait_ge(S("sp_plus1"), 1)
        A_(sp1, sp1, ACT.Ln).then_inc(S("ln_ready"), 1)
        act.wait_ge(S("qraw_free"), 1)
        store(A["qlast"][:], qlast[:])
        between(2)

        act.wait_ge(S("s_gd"), 4)
        ch = Chain(act, "act_s")
        ch.step(A_(sw[:, S_E], ps[4][:, 0:4 * SAMPLE], ACT.Exp))
        ch.step(A_(sw[SL, S_D], sw[SL, S_D], ACT.Exp))
        between(4)
        between()
        for n in range(1, 3):
            act.wait_ge(S("s_ax"), n + 1)
            A_(sw[SL, S_P], ps[4][SL, 0:4 * SAMPLE], ACT.Copy).then_inc(S("s_p"), 1)
            between(2)
        between()
        act.wait_ge(S("s_ztt"), 1)
        A_(sz[SL], ps[7][SL, :], ACT.Copy).then_inc(S("s_z"), 1)
        between(2)
        act.wait_ge(S("s_o"), 1)
        A_(qkv[:, 2 * HEADS:, ST], tiled(ps[5][:, 0:4 * SAMPLE], SAMPLE), ACT.Copy).then_inc(S("s_otaken"), 1)
        between()
        for h in range(HEADS):
            act.wait_ge(S("s_new"), 3 * (h + 1))
            act.dma_start(A["sdelta_out"][:, h], sst[h][:])\
                .then_inc(S("states_out" if h < HEADS - 1 else "last_state_out"), 16)
            between()

        for pr in range(2):
            b0 = (ps[4], ps[6])
            for hh in range(2):
                act.wait_ge(S("gd"), TILES * at_head(pr, hh))
                A_(dl[:, hh, P_], b0[hh][:, :], ACT.Exp).then_inc(S("egrow"), 1)
                A_(dl[:, hh, W_], dl[:, hh, W_], ACT.Exp).then_inc(S("decay"), 1)
            between(3)
            act.wait_ge(S("last_state_out"), 16)
            for hh in range(2):
                act.wait_ge(S("vt"), at_head(pr, hh))
                A_(dl[:, hh, V_], b0[hh][:, :], ACT.Copy).then_inc(S("vt_taken"), 1)
            between(2)
            for n in range(1, len(LEVELS)):
                for hh in range(2):
                    act.wait_ge(S("ax"), at_level(pr, n, hh))
                    A_(dl[:, hh, P_], b0[hh][:, :], ACT.Copy).then_inc(S("p_ready"), 1)
                between(2)
            for c in range(TILES):
                between(2)
                for hh in range(2):
                    act.wait_ge(S("o_done"), at_tile(pr, c, hh))
                    A_(qkv[:, 2 * HEADS + 2 * pr + hh, c * P:(c + 1) * P], b0[hh][:, 0:P], ACT.Copy)\
                        .then_inc(S("o_taken"), 1)
                between()
        act.wait_ge(S("s_new_p"), at_tile(1, TILES - 1, 1))
        store(A["pdelta_out"][:], pst[:])
        act.wait_ge(taken[1], O_GLU // 2 + CT)
        for j in range(CT):
            store(A["pconv"][:, j], u[:, j, SEQ:UP])
            store(A["sconv"][:, j], u_s(j)[:, :, DEC_SEQ:])
        between(FILL * SLICES)

        act.wait_ge(S("cv_taps"), 2 * CT * CONV_K)
        for j in range(CT):
            if j == 0:
                act.wait_ge(S("o_taken"), at_tile(1, TILES - 1, 1))
            if j >= 2:
                act.wait_ge(S("cv_avg"), j - 1)
            A_(tmp[:, j % 2], cv[:, j], ACT.Square).then_inc(S("cv_sq"), 1)
        for h in range(HEADS):
            if h >= 2:
                act.wait_ge(S("rms_avg"), h - 1)
            A_(sig[:, h % 2], qkv[:, 2 * HEADS + h], ACT.Square).then_inc(S("rms_sq"), 1)
        act.wait_ge(S("cv_var"), 1)
        A_(nrm[0:8, 1], nrm[0:8, 1], ACT.Sqrt, bias=eps_rows).then_inc(S("cv_root"), 1)
        act.wait_ge(stored, 16 * (2 + 2 * CT))
        for j in range(CT):
            act.wait_ge(S("cv_norm"), j + 1)
            if j == 0:
                act.wait_ge(S("rms_avg"), HEADS)
            if j >= 2:
                act.wait_ge(S("cv_silu"), j - 1)
            A_(sig[:, j % 2], cv[:, j], ACT.Sigmoid).then_inc(S("cv_sig"), 1)
            act.wait_ge(S("cv_silu"), j + 1)
            A_(z[0][:, j], cv[:, j], ACT.Copy).then_inc(S("z_hi"), 1)
        for h in range(HEADS):
            act.wait_ge(S("rms_out"), h + 1)
            A_(z[0][:, CT + h], qkv[:, 2 * HEADS + h], ACT.Copy).then_inc(S("z_hi"), 1)

        def gate_b(c, m, again=0):
            act.wait_ge(gemm_done, again * RING + c + 1)
            if not (isinstance(again, int) and m < 2):
                act.wait_ge(S("mixed"), again * 2 + m - 1)
            for h, half in enumerate(HALVES):
                ins = A_(gb[:, m % 2, half], out_pair(m)[h][:, 0:HALF], ACT.Sigmoid)
            ins.then_inc(taken[m % 2], 1)
            split(c + RING, again * 2)

        def mixed_hi(c, m, again=0):
            mm = m if isinstance(again, int) else act.snap(again * 2 + m)
            act.wait_ge(gemm_done, again * RING + c + 1)
            split(c + RING, again * 2)
            act.wait_ge(S("mixed"), mm + 1)
            A_(mixed[0][:, bass.ds(mm, 1)], mx[:, m % 2, 0:1], ACT.Copy).then_inc(S("mixed_hi"), 1)

        act.wait_ge(S("z_lo"), KB)
        gate_b(C_MIX, 0)
        gate_b(C_MIX + 1, 1)
        with act.Fori(0, 3) as it:
            for n in range(2):
                mixed_hi(C_MIX + 2 + 2 * n, n, it)
                gate_b(C_MIX + 3 + 2 * n, n + 2, it)
        mixed_hi(C_MIX + 14, 6)
        mixed_hi(C_MIX + 15, 7)

        def squares(name, c0):
            with act.Fori(0, 2) as g:
                for s in range(RING):
                    j = act.snap(g * RING + s)
                    act.wait_ge(gemm_done, g * RING + c0 + s + 1)
                    split(c0 + RING + s, 2 * g)
                    act.wait_ge(*ln(name, "res", KB, j + 1))
                    A_(lnt[:, s % 2], res[:, bass.ds(j, 1)].rearrange("p o t -> p (o t)"), ACT.Square)\
                        .then_inc(S("ln_sq"), 1)

        def ln_root(name):
            act.wait_ge(*ln(name, "var", 1, 1))
            A_(lns[:, 1], lns[:, 1], ACT.Sqrt, bias=eps_ln).then_inc(S("ln_root"), 1)

        def ln_affine(name, g, b, j, out):
            act.wait_ge(*ln(name, "norm", 2 * KB, 2 * (j + 1)))
            A_(res[:, j], res[:, j], ACT.Identity, bias=pc(b, j), scale=pc(g, j)).then_inc(S("ln_aff"), 1)
            act.wait_ge(*ln(name, "aff", KB, j + 1))
            if out is not None:
                A_(out[0][:, j], res[:, j], ACT.Copy).then_inc(S("ln_hi"), 1)

        squares("ln1", C_WO)
        act.wait_ge(S("mem_loaded"), 16)
        for kb in range(KB):
            A_(mem[0][:, kb], memraw[:, kb], ACT.Copy).then_inc(S("mem_hi"), 1)
        for i in range(KB):
            c = C_MEM + i
            act.wait_ge(gemm_done, c + 1)
            A_(mk[:, i], out_pair(i)[0][:, 0:N_MEM], ACT.Copy).then_inc(taken[i % 2], 1)
            split(c + RING)
            if i == 4:
                ln_root("ln1")
            if i > 4:
                ln_affine("ln1", "g1", "b1", i - 5, h1)
        for i in range(0, KB, 2):
            c = C_MEM + KB + i
            act.wait_ge(gemm_done, c + 2)
            for mb in range(2):
                A_(mv[:, mb, i * P:(i + 2) * P], out_pair(mb)[0][:, 0:2 * P], ACT.Copy).then_inc(taken[mb], 1)
            split(c + RING)
            split(c + RING + 1)
            for j in range(3 + i, min(5 + i, KB)):
                ln_affine("ln1", "g1", "b1", j, h1)
        act.wait_ge(taken[0], (O_MEM + 2 * KB) // 2)
        act.wait_ge(taken[1], (O_MEM + 2 * KB) // 2)
        store(A["mk"][:], mk[:])
        store(A["mv"][:], mv[:])

        act.wait_ge(*ln("ln1", "out", KB, KB))
        with act.Fori(0, 2) as g:
            for s in range(RING):
                j = act.snap(g * RING + s)
                act.wait_ge(gemm_done, g * RING + C_XQ + s + 1)
                for h, half in enumerate(HALVES):
                    ins = A_(aq[:, bass.ds(j, 1), half], out_pair(s)[h][:, 0:HALF].unsqueeze(1), ACT.Copy,
                             scale=X_DIM ** -0.5)
                ins.then_inc(taken[s % 2], 1)
                split(C_XQ + RING + s, 2 * g)

        def exps(h):
            act.wait_ge(S("att_max"), 3 * (h + 1) + (2 if h == 3 else 0))
            if h:
                act.wait_ge(S("att_flip"), h)
            for t in range(TILES):
                A_(ap[:, t], ps[t // 2][:, (t % 2) * N_MEM:(t % 2 + 1) * N_MEM], ACT.Exp, bias=amax[:, t:t + 1],
                   accum_out=asum[:, t:t + 1]).then_inc(S("att_exp"), 1)

        def flipped(h):
            act.wait_ge(S("att_flip"), h + 1)
            if h:
                act.wait_ge(S("att_o"), h)
            for mb in range(2):
                A_(apt[:, mb], ps[4 + mb][:, :], ACT.Copy).then_inc(S("att_pt"), 1)

        def out_hi(h):
            act.wait_ge(S("att_o"), h + 1)
            for d in range(2):
                A_(ao[0][:, 2 * h + d, PT], ps[6 + d][:, :], ACT.Copy).then_inc(S("ao_hi"), 1)

        exps(0)
        flipped(0)
        exps(1)
        out_hi(0)
        act.wait_ge(S("kv_used"), DEC_BATCH)
        A_(ssc[:], ps[2][:, :].rearrange("p (m c) -> p m c", m=2), ACT.Copy).then_inc(S("ssc_ready"), 1)
        flipped(1)
        exps(2)
        out_hi(1)
        act.wait_ge(S("att_max"), 3 * 3 + 2)
        for g in range(2):
            A_(aps[:, g], ps[3][:, g * N_MEM:(g + 1) * N_MEM], ACT.Exp, bias=samax[:, g:g + 1],
               accum_out=sasum[:, g:g + 1]).then_inc(S("att_exp"), 1)
        flipped(2)
        exps(3)
        act.wait_ge(S("sp_flip"), 1)
        A_(ssc[:], ps[2][:, :].rearrange("p (m c) -> p m c", m=2), ACT.Copy).then_inc(S("spt_ready"), 1)
        out_hi(2)
        flipped(3)
        act.wait_ge(S("kv_used"), 2 * DEC_BATCH)
        A_(ao[0][:, :, ST], tiled(ps[3][:, :], SAMPLE), ACT.Copy).then_inc(S("ao_hi"), 1)
        out_hi(3)

        squares("ln2", C_XO)
        ln_root("ln2")
        for j in range(KB):
            ln_affine("ln2", "g2", "b2", j, h2)

        def quarter(q, last=False):
            for n in range(2 * KB):
                c = C_FF + n
                act.wait_ge(gemm_done, q * (2 * KB) + c + 1)
                if n < KB:
                    if n >= 2:
                        act.wait_ge(S("hid_lo"), q * KB + n - 1)
                    for h, half in enumerate(HALVES):
                        ins = A_(ht[:, n % 2, half], out_pair(n)[h][:, 0:HALF], ACT.Relu)
                    ins.then_inc(taken[n % 2], 1)
                    act.wait_ge(taken[n % 2], q * KB + (O_FF + n) // 2 + 1)
                    A_(hid[0][:, n], ht[:, n % 2], ACT.Square).then_inc(S("hid_hi"), 1)
                if not (last and n >= 2 * KB - RING):
                    split(c + RING, q * KB)
                if last and n >= KB:
                    j = n - KB
                    act.wait_ge(S("acc"), q * KB + j + 1)
                    act.wait_ge(taken[j % 2], q * KB + (O_FF + KB + j) // 2 + 1)
                    A_(lnt[:, j % 2], res[:, j], ACT.Square).then_inc(S("ln_sq"), 1)
        act.wait_ge(S("acc_ready"), KB)
        act.wait_ge(stored, 16 * (4 + 2 * CT))
        with act.Fori(0, QUARTERS - 1) as q:
            quarter(q)
        quarter(QUARTERS - 1, True)
        ln_root("ln3")
        for j in range(KB):
            ln_affine("ln3", "g3", "b3", j, None)
            store(A["yT"][:, j], res[:, j])

    @block.vector
    def _(dve):
        V = nc.vector

        for kb in range(KB):
            dve.wait_ge(S("x_hi"), kb + 1)
            V.tensor_tensor(x[1][:, kb], xraw[:, kb], x[0][:, kb].bitcast(f32), sub).then_inc(S("x_lo"), 1)
        dve.wait_ge(S("bdw_split"), 1)
        V.tensor_tensor(bdw[1][:], wbd[:], bdw[0][:].bitcast(f32), sub).then_inc(S("bdw_split"), 1)
        dve.wait_ge(S("x_lo"), KB)
        dve.wait_ge(S("par_loaded"), 48)
        V.memset(qraw[:, :, 0:QH], 0.0).then_inc(S("q_pad"), 1)
        V.tensor_copy(qraw[:, :, RP:].rearrange("p j (b t) -> p j b t", t=RS)[:, :, :, 0:QH],
                      qhist[:].rearrange("p j (b t) -> p j b t", t=QH)).then_inc(S("q_pad"), 1)
        def conv_taps(ch, weight, src_p, src_s, dst_p, dst_s, taps, bias=None):
            for k in taps:
                for src, dst in ((src_p, dst_p), (src_s, dst_s)):
                    ch.wait(1)
                    w = weight(k)
                    if k == 0:
                        ins = V.tensor_scalar(dst, src(k), w, bias, mul, add if bias is not None else ALU.bypass)
                    else:
                        ins = V.scalar_tensor_tensor(dst, src(k), w, dst, mul, add)
                    ch.step(ins)

        with dve.Fori(0, QT // RING) as g:
            for s in range(RING):
                j = dve.snap(g * RING + s)
                ch = Chain(dve, "q_conv", g * (8 * RING) + 8 * s)
                dve.wait_ge(taken[s % 2], g * 2 + s // 2 + 1)
                row = qraw[:, bass.ds(j, 1)]
                out = qkv[:, bass.ds(j, 1)]
                wcol = dve.snap(j * SHORT_K + PAR["w_short"])
                conv_taps(ch, lambda k: par[:, bass.ds(wcol + k, 1)],
                          lambda k: row[:, :, k:k + SEQ].rearrange("p o t -> p (o t)"),
                          lambda k: row[:, :, RP:].rearrange("p o (b t) -> p (o b) t", t=RS)[:, :, k:k + DEC_SEQ],
                          out[:, :, PT].rearrange("p o t -> p (o t)"),
                          out[:, :, ST].rearrange("p o (b t) -> p (o b) t", t=DEC_SEQ), range(SHORT_K))
                ch.wait()
                dve.wait_ge(S("q_sig"), g * RING + s + 1)
                o = out.rearrange("p o t -> p (o t)")
                V.tensor_tensor(o, o, sig[:, s % 2], mul).then_inc(S("q_silu"), 1)
        V.tensor_copy(qlast[:, :, 0:QH], qraw[:, :, SEQ:RP]).then_inc(S("q_last"), 1)
        V.tensor_copy(qlast[:, :, QH:].rearrange("p j (b t) -> p j b t", t=QH),
                      qraw[:, :, RP:].rearrange("p j (b t) -> p j b t", t=RS)[:, :, :, DEC_SEQ:]).then_inc(S("qraw_free"), 1)

        dve.wait_ge(S("consts"), CONSTS)
        dve.wait_ge(S("cst_loaded"), 16 * (2 + CT))
        chc = Chain(dve, "cv_taps")
        todo = [(j, k) for j in range(CT) for k in range(CONV_K)]

        def wide_taps(n, blocks):
            while n and todo and todo[0][0] < blocks:
                j, k = todo.pop(0)
                conv_taps(chc, lambda kk: pc("w_dw", j * CONV_K + kk), lambda kk: u[:, j, kk:kk + SEQ],
                          lambda kk: u_s(j)[:, :, kk:kk + DEC_SEQ], cv[:, j, PT], tiled(cv[:, j, ST], DEC_SEQ), [k],
                          bias=pc("b_dw", j))
                n -= 1

        def filler():
            blocks = 0
            for f in range(FILL):
                c, o = C_GLU + f, O_GLU + f
                for _ in range(SLICES - 1):
                    wide_taps(2, blocks)
                    yield
                if c < C_OG and f % 2:
                    i = f // 2
                    dve.wait_ge(taken[0], O_GLU // 2 + i + 1)
                    dve.wait_ge(gemm_done, c + 1)
                    lo, hi = out_pair(1)
                    bias = pc("b_glu", i)
                    V.scalar_tensor_tensor(u[:, i, CH:CH + HALF], lo[:, 0:HALF], bias, sig[:, i % 2, 0:HALF], add, mul)
                    V.scalar_tensor_tensor(u[:, i, CH + HALF:UP], hi[:, 0:SEQ - HALF], bias, sig[:, i % 2, HALF:SEQ],
                                           add, mul)
                    V.scalar_tensor_tensor(u_s(i)[:, :, CH:], tiled(hi[:, SEQ - HALF:HALF], DEC_SEQ), bias,
                                           tiled(sig[:, i % 2, ST], DEC_SEQ), add, mul).then_inc(taken[1], 1)
                    dve.wait_ge(taken[1], O_GLU // 2 + i + 1)
                    blocks += 1
                elif C_OG <= c < C_GA:
                    i = c - C_OG
                    dve.wait_ge(S("og_sig"), i + 1)
                    for h, half in enumerate(HALVES):
                        ins = V.tensor_tensor(sgate[:, i, half], out_pair(o)[h][:, 0:HALF], sig[:, i % 2, half], mul)
                    ins.then_inc(taken[o % 2], 1)
                wide_taps(2, blocks)
                yield

        fill = filler()

        def between(n=1):
            for _ in range(n):
                next(fill, None)

        own = ch = Chain(dve, "dve_own")
        dve.wait_ge(S("par_loaded"), 48)
        ch(V.memset(bd, 0.0))
        dve.wait_ge(S("bd_flip"), 1)
        V.tensor_copy(bd[:, 0:TILES], ps[6][:, 0:32].rearrange("p (t c) -> p t c", c=8))
        ch(V.tensor_copy(bd[SL, TILES], ps[6][SL, 32:40]))
        ch(V.tensor_tensor(sp0, bd[:, :, 4:8], rep(par[:, PAR["dt_bias"]:PAR["dt_bias"] + 4], 5), add))
        ch(V.tensor_scalar(sp1, sp0, -1.0, None, mul))
        ch(V.tensor_tensor(sp1, sp0, sp1, ALU.min))

        dve.wait_ge(S("l2_root"), 2)
        V.reciprocal(l2r[0:8, 0], l2r[0:8, 0]).then_inc(S("l2_inv"), 1)
        between(2)
        ch = own
        dve.wait_ge(S("exp_ready"), 1)
        V.tensor_scalar(sp1, sp1, 1.0, None, add).then_inc(S("sp_plus1"), 1)
        ch(V.tensor_scalar(nega, nega, -1.0, None, mul))
        ch(V.tensor_scalar(sp0, sp0, 0.0, None, ALU.max))
        dve.wait_ge(S("ln_ready"), 1)
        ch(V.tensor_tensor(sp0, sp0, sp1, add))
        V.tensor_tensor(ld, sp0, rep(nega, 5), mul).then_inc(S("ld_ready"), 1)
        dve.wait_ge(S("g_done"), 1)
        V.tensor_copy(gcol[SL, TILES], ps[7][SL, 80:84])
        V.tensor_copy(gcol[:, 0:TILES], ps[7][:, 64:80].rearrange("p (t c) -> p t c", c=4))\
            .then_inc(S("gcol_ready"), 1)
        for i in range(2 * HEADS):
            dve.wait_ge(S("l2_bc"), i + 1)
            for h, half in enumerate(HALVES):
                ins = V.scalar_tensor_tensor(qkv[:, i, half], ps[6 - 2 * (i % 2) + h][:, 0:HALF],
                                             DK ** -0.5 if i < HEADS else 1.0, qkv[:, i, half], mul, mul)
            ins.then_inc(S("l2_done"), 1)
        between(2)

        dve.wait_ge(S("gcol_ready"), 1)
        dve.wait_ge(S("ld_ready"), 1)
        dve.wait_ge(S("l2_done"), 2 * HEADS)
        dve.wait_ge(stored, 16)
        dve.wait_ge(S("beta_ready"), 1)
        V.tensor_copy(sld[SL], bc(ld[SL, TILES], DK)).then_inc(S("sld_ready"), 1)
        V.memset(pst[:], 0.0).then_inc(S("pst_zero"), 1)
        dve.wait_ge(S("s_grow"), 1)
        for h in range(HEADS):
            V.tensor_scalar(sw[SL, S_D, h], ps[4][SL, h * SAMPLE:(h + 1) * SAMPLE], gcol[SL, TILES, h:h + 1], 0.0,
                            sub, ALU.min).then_inc(S("s_gd"), 1)
        dve.wait_ge(S("act_s"), 2)
        D, E = sw[SL, S_D], sw[:, S_E]
        ch(V.tensor_tensor(D, D, rep(triu8[SL], HEADS), mul))
        ch.step(V.tensor_reduce(stail[SL], D.rearrange("p h (b t) -> p h b t", t=DEC_SEQ)[:, :, :, DEC_SEQ - 1], X, add))
        ch.step(V.tensor_copy(seglast, E.rearrange("p h (b t) -> p h b t", t=DEC_SEQ)[:, :, :, DEC_SEQ - 1]))
        dve.wait_ge(S("s_kk"), 1)
        ch(V.tensor_tensor(sw[SL, S_NB], tiled(ps[5][SL, 0:256], SAMPLE), D, mul))
        ch(V.tensor_tensor(sw[SL, S_NB], sw[SL, S_NB], bc(beta[SL, TILES], SAMPLE), mul))
        ch.step(V.tensor_tensor(sw[SL, S_QK], tiled(ps[5][SL, 256:512], SAMPLE), D, mul))
        dve.wait_ge(S("s_kt"), 1)
        ch(V.tensor_tensor(skt[SL], tiled(ps[6][SL, :]), bc(stail[SL], DK), mul))
        V.tensor_tensor(qkv[:, 0:HEADS, ST], qkv[:, 0:HEADS, ST], E, mul).then_inc(S("s_scaled"), 1)
        V.tensor_tensor(qkv[:, HEADS:2 * HEADS, ST], qkv[:, HEADS:2 * HEADS, ST], E, mul).then_inc(S("s_scaled"), 1)
        between(4)
        for n in range(3):
            if n:
                dve.wait_ge(S("s_ax"), n)
                dve.wait_ge(S("s_xy"), 2 * n)
            V.tensor_tensor(sw[SL, S_W], sw[SL, S_NB], rep(lmask[SL, n, SL], HEADS), mul).then_inc(S("s_as"), 1)
            if n:
                between()
            if n == 0:
                dve.wait_ge(S("s_as"), 1)
                dve.wait_ge(S("s_ax"), 1)
                V.tensor_tensor(sw[SL, S_X], rep(ident[SL, SL], HEADS), tiled(ps[4][SL, 0:256], SAMPLE), sub)\
                    .then_inc(S("s_xy"), 1)
                V.tensor_tensor(sw[SL, S_Y], rep(ident[SL, SL], HEADS), sw[SL, S_W], sub).then_inc(S("s_xy"), 1)
            else:
                dve.wait_ge(S("s_xax"), n)
                for i, k in enumerate((S_X, S_Y)):
                    V.tensor_tensor(sw[SL, k], sw[SL, k], tiled(ps[5][SL, 256 * i:256 * (i + 1)], SAMPLE), sub)\
                        .then_inc(S("s_xy"), 1)
                dve.wait_ge(S("s_xy"), 2 * (n + 1))
            between()
        dve.wait_ge(S("s_ks"), 1)
        V.tensor_tensor(szt[:], qkv[:, 2 * HEADS:, ST], tiled(ps[6][:, 0:256], SAMPLE), sub).then_inc(S("s_zt"), 1)
        between(2)
        dve.wait_ge(S("s_yz"), 1)
        V.tensor_tensor(su[SL], tiled(ps[4][SL, :]), bc(beta[SL, TILES], DK), mul).then_inc(S("s_u"), 1)
        between(2)
        ch.wait()
        for h in range(HEADS):
            if h:
                dve.wait_ge(S("s_ds"), h)
            V.tensor_tensor(sktm[SL], rep(skt[SL, h], DEC_BATCH), bc(same8[SL], DK), mul).then_inc(S("s_ktm"), 1)
            if h == 0:
                dve.wait_ge(S("s_o"), 1)
            V.tensor_tensor(sst[h][:], sst[h][:], bc(seglast[:, h], DK), mul).then_inc(S("s_new"), 1)
            dve.wait_ge(S("s_new"), 3 * h + 1)
            dve.wait_ge(S("s_ds"), h + 1)
            for i in range(2):
                half = sst[h][:, 4 * i:4 * i + 4]
                V.tensor_tensor(half, half, tiled(ps[6 + i][:, :]), add).then_inc(S("s_new"), 1)
            between()

        dve.wait_ge(S("s_otaken"), 1)
        dve.wait_ge(S("s_new"), 3 * HEADS)
        dve.wait_ge(S("states_out"), 16 * (HEADS - 1))
        for pr in range(2):
            b0, b1 = (ps[4], ps[6]), (ps[5], ps[7])
            for hh in range(2):
                if pr:
                    dve.wait_ge(S("o_done"), at_tile(0, TILES - 1, hh))
                    dve.wait_ge(S("ku"), at_tile(0, TILES - 1, hh))
                V.tensor_copy(dt(hh, X_), bc(ld[:, 0:TILES, 2 * pr + hh], P)).then_inc(S("ldb"), 1)
            for hh in range(2):
                h = 2 * pr + hh
                dve.wait_ge(S("grow"), at_head(pr, hh))
                for c in range(TILES):
                    V.tensor_scalar(dt(hh, W_)[:, c], b0[hh][:, c * P:(c + 1) * P], gcol[:, c, h:h + 1], 0.0, sub,
                                    ALU.min).then_inc(S("gd"), 1)
            between()
            for hh in range(2):
                h = 2 * pr + hh
                dve.wait_ge(S("decay"), at_head(pr, hh))
                D, E = dt(hh, W_), dt(hh, P_)
                ch(V.tensor_tensor(D, D, rep(triu, TILES), mul))
                ch.step(V.tensor_copy(etail[:, hh], D[:, :, P - 1]))
                ch.step(V.tensor_copy(eglast[:, hh], E[:, :, P - 1]))
                dve.wait_ge(S("kk"), at_head(pr, hh))
                V.tensor_tensor(dt(hh, NB_), tiled(b1[hh][:, :]), D, mul).then_inc(S("nb_raw"), 1)
                dve.wait_ge(S("nb_raw"), at_head(pr, hh))
                ch.step(V.tensor_tensor(dt(hh, NB_), dt(hh, NB_), bc(beta[:, 0:TILES, h], P), mul))
                dve.wait_ge(S("qk"), at_head(pr, hh))
                V.tensor_tensor(dt(hh, QK_), tiled(b0[hh][:, :]), D, mul).then_inc(S("qk_taken"), 1)
            between(2)
            for hh in range(2):
                h = 2 * pr + hh
                dve.wait_ge(S("kt"), at_head(pr, hh))
                dve.wait_ge(S("last_state_out"), 16)
                ch.wait()
                ch.step(V.tensor_tensor(dt(hh, K_), tiled(b1[hh][:, :]), bc(etail[:, hh], P), mul))
                for w in (HEADS + h, h):
                    V.tensor_tensor(qkv[:, w, PT], qkv[:, w, PT], dl[:, hh, P_], mul).then_inc(S("scaled"), 1)
            between()
            def blocks_of(n):
                for hh in range(2):
                    if n:
                        dve.wait_ge(S("ax"), at_level(pr, n - 1, hh))
                    else:
                        dve.wait_ge(S("qk_taken"), at_head(pr, hh))
                    V.tensor_tensor(dt(hh, W_), dt(hh, NB_), rep(lmask[:, n], TILES), mul).then_inc(S("as_ready"), 1)

            blocks_of(0)
            for hh in range(2):
                dve.wait_ge(S("as_ready"), at_level(pr, 0, hh))
                V.tensor_tensor(dt(hh, Y_), rep(ident, TILES), dt(hh, W_), sub).then_inc(S("xy"), 1)
                dve.wait_ge(S("ax"), at_level(pr, 0, hh))
                V.tensor_tensor(dt(hh, X_), rep(ident, TILES), tiled(b0[hh][:, :]), sub).then_inc(S("xy"), 1)
            dve.wait_ge(S("xy"), 2 * at_level(pr, 0, 1))
            blocks_of(1)
            between()
            for n in range(1, len(LEVELS)):
                between()
                for hh in range(2):
                    dve.wait_ge(S("xy"), 2 * at_level(pr, n - 1, hh))
                    if n < len(LEVELS) - 1:
                        dve.wait_ge(S("xax"), (pr * 5 + n - 1) * 2 + hh + 1)
                        V.tensor_tensor(dt(hh, X_), dt(hh, X_), tiled(b1[hh][:, :]), sub).then_inc(S("xy"), 1)
                        dve.wait_ge(S("yay"), (pr * 6 + n - 1) * 2 + hh + 1)
                        V.tensor_tensor(dt(hh, Y_), dt(hh, Y_), tiled(b0[hh][:, :]), sub).then_inc(S("xy"), 1)
                    else:
                        dve.wait_ge(S("yay"), (pr * 6 + n - 1) * 2 + hh + 1)
                        V.tensor_tensor(dt(hh, Y_), dt(hh, Y_), tiled(b0[hh][:, :]), sub).then_inc(S("xy"), 2)
                if n < len(LEVELS) - 1:
                    blocks_of(n + 1)
                between()
            for c in range(TILES):
                for hh in range(2):
                    dve.wait_ge(S("ks"), at_tile(pr, c, hh))
                    V.tensor_tensor(dt(hh, P_)[:, c], dt(hh, V_)[:, c], b0[hh][:, 0:DK], sub).then_inc(S("z_ready"), 1)
                between()
                for hh in range(2):
                    dve.wait_ge(S("yz"), at_tile(pr, c, hh))
                    V.tensor_scalar(dt(hh, W_)[:, c], b1[hh][:, 0:DK], beta[:, c, 2 * pr + hh:2 * pr + hh + 1], None,
                                    mul).then_inc(S("u_ready"), 1)
                between()
                for hh in range(2):
                    state = pst[:, 2 * pr + hh]
                    dve.wait_ge(S("ku"), at_tile(pr, c, hh))
                    dve.wait_ge(S("o_done"), at_tile(pr, c, hh))
                    V.scalar_tensor_tensor(state, state, eglast[:, hh, c:c + 1], b1[hh][:, 0:DK], mul, add)\
                        .then_inc(S("s_new_p"), 1)
                between()
        between(FILL * SLICES)
        wide_taps(len(todo), CT)
        chc.wait()

        def variance(ch, mean, var, work, rows=slice(0, P)):
            for h, half in enumerate(HALVES):
                ch(V.tensor_copy(mean[:, half], ps[4 + h][rows, 0:HALF]))
            ch(V.tensor_tensor(work, mean, mean, mul))
            for h, half in enumerate(HALVES):
                ch(V.tensor_tensor(var[:, half], ps[6 + h][rows, 0:HALF], work[:, half], sub))
            return V.tensor_scalar(var, var, 0.0, None, ALU.max)

        dve.wait_ge(S("rms_avg"), HEADS)
        variance(ch, nrm[0:8, 0], nrm[0:8, 1], tmp[0:8, 0], slice(0, 8)).then_inc(S("cv_var"), 1)
        dve.wait_ge(S("cv_root"), 1)
        V.reciprocal(nrm[0:8, 1], nrm[0:8, 1]).then_inc(S("n_inv"), 1)
        dve.wait_ge(S("n_bc"), 1)
        for j in range(CT):
            for h, half in enumerate(HALVES):
                ch.step(V.tensor_tensor(cv[:, j, half], cv[:, j, half], ps[4 + h][:, 0:HALF], sub))
            for h, half in enumerate(HALVES):
                ch.wait(1)
                ch.step(V.tensor_tensor(cv[:, j, half], cv[:, j, half], ps[6 + h][:, 0:HALF], mul))
            ch.wait()
            V.tensor_scalar(cv[:, j], cv[:, j], pc("cg", j), pc("cb", j), mul, add).then_inc(S("cv_norm"), 1)

        def z_lo(j, src):
            dve.wait_ge(S("z_hi"), j + 1)
            V.tensor_tensor(z[1][:, j], src, z[0][:, j].bitcast(f32), sub).then_inc(S("z_lo"), 1)

        for h in range(HEADS):
            dve.wait_ge(S("cv_sig"), h + 1)
            V.tensor_tensor(cv[:, h], cv[:, h], sig[:, h % 2], mul).then_inc(S("cv_silu"), 1)
            o = qkv[:, 2 * HEADS + h]
            dve.wait_ge(S("n_bc"), h + 2)
            for i, half in enumerate(HALVES):
                ch.step(V.scalar_tensor_tensor(o[:, half], ps[4 + 2 * (h % 2) + i][:, 0:HALF], pc("dng"), o[:, half],
                                               mul, mul))
            ch.wait()
            V.tensor_tensor(o, o, sgate[:, h], mul).then_inc(S("rms_out"), 1)
            z_lo(h, cv[:, h])
        V.engine_nop().then_inc(S("mix_free"), 1)
        for h in range(HEADS):
            z_lo(CT + h, qkv[:, 2 * HEADS + h])
        dve.wait_ge(S("z_lo"), KB)

        def mix(c, m, again=0):
            mm = m if isinstance(again, int) else dve.snap(again * 2 + m)
            ch = Chain(dve, "dve_mix", again * 4 + 2 * m)
            dve.wait_ge(gemm_done, again * RING + c + 1)
            dve.wait_ge(taken[m % 2], again + O_GB // 2 + m // 2 + 1)
            a, b = mx[:, m % 2, 0:1], mx[:, m % 2, 1:2]
            for h, half in enumerate(HALVES):
                ch.step(V.tensor_tensor(a[:, :, half], ps[4 + h][:, 0:HALF].unsqueeze(1),
                                        sga[:, bass.ds(mm, 1), half], mul))
            V.tensor_tensor(b[:, 0, HALVES[0]], ps[6][:, 0:HALF], gb[:, m % 2, HALVES[0]], mul)
            V.tensor_tensor(b[:, 0, HALVES[1]], ps[7][:, 0:HALF], gb[:, m % 2, HALVES[1]], mul)\
                .then_inc(S("mix_free"), 1)
            ch.wait()
            dve.wait_ge(S("mix_free"), mm + 2)
            V.tensor_tensor(a, a, b, add).then_inc(S("mixed"), 1)
            dve.wait_ge(S("mixed_hi"), mm + 1)
            V.tensor_tensor(mixed[1][:, bass.ds(mm, 1)], a, mixed[0][:, bass.ds(mm, 1)].bitcast(f32), sub)\
                .then_inc(S("mixed_lo"), 1)

        with dve.Fori(0, 3) as it:
            for n in range(2):
                mix(C_MIX + 2 + 2 * n, n, it)
        mix(C_MIX + 14, 6)
        mix(C_MIX + 15, 7)

        def residual(name, c0, o0, old):
            V.memset(lns[:], 0.0).then_inc(S("ln_zero"), 1)
            dve.wait_ge(*ln(name, "zero", 1, 1))
            with dve.Fori(0, 2) as g:
                for s in range(RING):
                    j = dve.snap(g * RING + s)
                    r = res[:, bass.ds(j, 1)]
                    ch = Chain(dve, name + "_t", g * RING + s)
                    dve.wait_ge(gemm_done, g * RING + c0 + s + 1)
                    for h, half in enumerate(HALVES):
                        ins = V.scalar_tensor_tensor(r[:, :, half], old[0][:, bass.ds(j, 1), half].bitcast(f32), ALPHA,
                                                     out_pair(s)[h][:, 0:HALF].unsqueeze(1), mul, add)
                        if h == 0:
                            ch.step(ins)
                    ins.then_inc(taken[s % 2], 1)
                    ch.wait()
                    dve.wait_ge(taken[s % 2], g * 2 + (o0 + s) // 2 + 1)
                    V.scalar_tensor_tensor(r, old[1][:, bass.ds(j, 1)].bitcast(f32), ALPHA, r, mul, add)\
                        .then_inc(S("ln_res"), 1)
                    dve.wait_ge(*ln(name, "res", KB, j + 1))
                    V.tensor_tensor(lns[:, 0:1], lns[:, 0:1], r, add).then_inc(S("ln_sum"), 1)
                    dve.wait_ge(*ln(name, "sq", KB, j + 1))
                    V.tensor_tensor(lns[:, 1], lns[:, 1], lnt[:, s % 2], add).then_inc(S("ln_sum"), 1)
                    dve.wait_ge(*ln(name, "sum", 2 * KB, g * (2 * RING) + 2 * s + 2))

        def normalise(name, out=None):
            ch = own
            dve.wait_ge(*ln(name, "avg", 1, 1))
            variance(ch, lns[:, 0], lns[:, 1], lnt[:, 0]).then_inc(S("ln_var"), 1)
            dve.wait_ge(*ln(name, "root", 1, 1))
            ch(V.reciprocal(lns[:, 1], lns[:, 1]))

            def lo(j):
                dve.wait_ge(*ln(name, "hi", KB, j + 1))
                V.tensor_tensor(out[1][:, j], res[:, j], out[0][:, j].bitcast(f32), sub).then_inc(S("ln_out"), 1)

            for j in range(KB):
                V.tensor_tensor(res[:, j], res[:, j], lns[:, 0], sub).then_inc(S("ln_norm"), 1)
                dve.wait_ge(*ln(name, "norm", 2 * KB, 2 * j + 1))
                V.tensor_tensor(res[:, j], res[:, j], lns[:, 1], mul).then_inc(S("ln_norm"), 1)
                if out is not None and j:
                    lo(j - 1)
            if out is not None:
                lo(KB - 1)

        residual("ln1", C_WO, O_WO, x)
        for kb in range(KB):
            dve.wait_ge(S("mem_hi"), kb + 1)
            V.tensor_tensor(mem[1][:, kb], memraw[:, kb], mem[0][:, kb].bitcast(f32), sub).then_inc(S("mem_lo"), 1)
        normalise("ln1", h1)


        ch = own

        def row_max(out, bank):
            V.tensor_reduce(out, bank[:, :].rearrange("p (t m) -> p t m", m=N_MEM), X, ALU.max)\
                .then_inc(S("att_max"), 1)

        def maxima(h):
            extra = 2 if h == 3 else 0
            dve.wait_ge(S("att_sc"), h + 1)
            if h:
                dve.wait_ge(S("att_exp"), TILES * h + extra)
            row_max(amax[:, 0:2], ps[0])
            row_max(amax[:, 2:4], ps[1])
            dve.wait_ge(S("att_max"), 3 * h + extra + 2)
            V.tensor_scalar(amax, amax, -1.0, None, mul).then_inc(S("att_max"), 1)

        def probs(h):
            dve.wait_ge(S("att_exp"), TILES * (h + 1) + (2 if h == 3 else 0))
            ch(V.reciprocal(asum, asum))
            V.tensor_tensor(ap[:], ap[:], bc(asum, N_MEM), mul).then_inc(S("att_p"), 1)

        def out_lo(h):
            for d in range(2):
                i = 2 * h + d
                dve.wait_ge(S("ao_hi"), i + 1 + (1 if h == 3 else 0))
                V.tensor_tensor(ao[1][:, i, PT], ps[6 + d][:, :], ao[0][:, i, PT].bitcast(f32), sub)\
                    .then_inc(S("ao_lo"), 1)

        for h in range(3):
            maxima(h)
            probs(h)
            if h:
                out_lo(h - 1)
        dve.wait_ge(S("ssc_flip"), 1)
        row_max(samax, ps[3])
        dve.wait_ge(S("att_max"), 3 * 3 + 1)
        V.tensor_scalar(samax, samax, -1.0, None, mul).then_inc(S("att_max"), 1)
        dve.wait_ge(S("att_exp"), TILES * 3 + 2)
        ch(V.reciprocal(sasum, sasum))
        V.tensor_tensor(aps[:], aps[:], bc(sasum, N_MEM), mul).then_inc(S("sp_ready"), 1)
        maxima(3)
        probs(3)
        out_lo(2)
        dve.wait_ge(S("ao_hi"), KB - 1)
        V.tensor_tensor(ao[1][:, :, ST], tiled(ps[3][:, :], SAMPLE), ao[0][:, :, ST].bitcast(f32), sub)\
            .then_inc(S("ao_lo"), 1)
        out_lo(3)

        residual("ln2", C_XO, O_XO, h1)
        normalise("ln2")
        for j in range(KB):
            dve.wait_ge(*ln("ln2", "out", KB, j + 1))
            V.tensor_scalar(res[:, j], res[:, j], ALPHA, None, mul).then_inc(S("acc_ready"), 1)

        dve.wait_ge(S("acc_ready"), KB)
        V.memset(lns[:], 0.0).then_inc(S("ln_zero"), 1)
        dve.wait_ge(*ln("ln3", "zero", 1, 1))

        def quarter(q, last=False):
            for n in range(KB):
                dve.wait_ge(taken[n % 2], q * KB + (O_FF + n) // 2 + 1)
                V.tensor_tensor(hs[:, n % 2], ht[:, n % 2], ht[:, n % 2], mul).then_inc(S("hid_sq"), 1)
                dve.wait_ge(S("hid_sq"), q * KB + n + 1)
                dve.wait_ge(S("hid_hi"), q * KB + n + 1)
                V.tensor_tensor(hid[1][:, n], hs[:, n % 2], hid[0][:, n].bitcast(f32), sub).then_inc(S("hid_lo"), 1)
            for j in range(KB):
                dve.wait_ge(gemm_done, q * (2 * KB) + C_FF + KB + j + 1)
                V.tensor_tensor(res[:, j, HALVES[0]], res[:, j, HALVES[0]], out_pair(j)[0][:, 0:HALF], add)\
                    .then_inc(S("acc"), 1)
                V.tensor_tensor(res[:, j, HALVES[1]], res[:, j, HALVES[1]], out_pair(j)[1][:, 0:HALF], add)\
                    .then_inc(taken[j % 2], 1)
                if last:
                    dve.wait_ge(S("acc"), q * KB + j + 1)
                    dve.wait_ge(taken[j % 2], q * KB + (O_FF + KB + j) // 2 + 1)
                    V.tensor_tensor(lns[:, 0], lns[:, 0], res[:, j], add).then_inc(S("ln_sum"), 1)
                    dve.wait_ge(*ln("ln3", "sq", KB, j + 1))
                    V.tensor_tensor(lns[:, 1], lns[:, 1], lnt[:, j % 2], add).then_inc(S("ln_sum"), 1)
                    dve.wait_ge(*ln("ln3", "sum", 2 * KB, 2 * (j + 1)))

        with dve.Fori(0, QUARTERS - 1) as q:
            quarter(q)
        quarter(QUARTERS - 1, True)
        normalise("ln3")

    block_ctx.__exit__(None, None, None)


def _blocks(v):
    return np.ascontiguousarray(v.reshape(-1, P).T)


def _rows(a):
    return np.ascontiguousarray(a.reshape(a.shape[0], -1, P).transpose(2, 1, 0))


def _chunks(w):
    return w.reshape(KB, P, -1, P).transpose(2, 1, 0, 3)


def _shape_constants():
    i = np.arange(P)
    ident = np.eye(P, dtype=np.float32)
    triu = (i[:, None] <= i[None, :]).astype(np.float32)
    j = np.arange(SAMPLE)
    triu8 = np.zeros((P, SAMPLE), np.float32)
    triu8[:SAMPLE] = (j[:, None] <= j[None, :]) & (j[:, None] // DEC_SEQ == j[None, :] // DEC_SEQ)
    same8 = np.zeros((P, DEC_BATCH), np.float32)
    same8[:SAMPLE] = j[:, None] // DEC_SEQ == np.arange(DEC_BATCH)[None, :]
    levels = np.stack([((i[:, None] // (2 * s) == i[None, :] // (2 * s)) & (i[None, :] // s % 2 == 1)
                        & (i[:, None] // s % 2 == 0)).astype(np.float32) for s in LEVELS], axis=1)
    return np.concatenate([ident, triu, triu8, same8], axis=1), np.ascontiguousarray(levels)


def kernel(**inputs):
    import concourse.bacc as _bacc
    from concourse.bass_utils import run_bass_kernel_spmd as _run

    a = {k: np.asarray(v) for k, v in inputs.items()}
    w_in = a["w_in"][0]
    cols = {}
    off = 0
    for name, width in (("glu", 1024), ("qkv", 1536), ("og", 512), ("bd", 8), ("ga", 1024), ("gb", 1024)):
        cols[name] = _chunks(w_in[:, off:off + width]) if name != "bd" else w_in[:, off:off + width]
        off += width
    out_ab = _chunks(np.concatenate([a["w_conv_out"][0], a["w_dn_out"][0]], axis=0))
    ff1, ff2 = _chunks(a["w_ff1"][0]), a["w_ff2"][0]
    order = [cols["qkv"]]
    for i in range(CT):
        order += [cols["glu"][CT + i:CT + i + 1], cols["glu"][i:i + 1]]
    order.append(cols["og"])
    order += [cols["ga"], cols["gb"][0:2]]
    for m in range(KB - 2):
        order += [out_ab[m:m + 1], cols["gb"][m + 2:m + 3]]
    order.append(out_ab[KB - 2:])
    order += [_chunks(a["w_o"][0]), _chunks(a["w_mem_kv"][0]), _chunks(a["w_xq"][0]), _chunks(a["w_xo"][0])]
    for q in range(QUARTERS):
        order += [ff1[KB * q:KB * (q + 1)], _chunks(ff2[D_MODEL * q:D_MODEL * (q + 1)])]
    vectors = {
        "b_glu": _blocks(a["b_glu"][0]), "b_dw": _blocks(a["b_dw"][0]), "cg": _blocks(a["ln_conv_g"][0]),
        "cb": _blocks(a["ln_conv_b"][0]), "dng": _blocks(a["dn_norm_g"][0]),
        "g1": _blocks(a["ln1_g"][0]), "b1": _blocks(a["ln1_b"][0]), "g2": _blocks(a["ln2_g"][0]),
        "b2": _blocks(a["ln2_b"][0]), "g3": _blocks(a["ln3_g"][0]), "b3": _blocks(a["ln3_b"][0]),
        "w_dw": _rows(a["w_dw"][0]).reshape(P, -1), "w_short": _rows(a["w_short"][0]).reshape(P, -1),
        "a_log": np.tile(a["a_log"], (P, 1)), "dt_bias": np.tile(a["dt_bias"], (P, 1)),
    }
    cst, levels = _shape_constants()
    mem = a["mem_prompt"][0]
    arrays = {
        "xT": _rows(np.concatenate([a["x_prompt"][0], a["x_sample"].reshape(SAMPLE, D_MODEL)], axis=0)),
        "w": np.concatenate(order, axis=0),
        "wbd": np.ascontiguousarray(cols["bd"].reshape(KB, P, 8).transpose(1, 0, 2)),
        "par": np.concatenate([vectors[n] for n, _ in WIDTHS], axis=1),
        "cst": cst, "lmask": levels,
        "qhist": np.ascontiguousarray(a["state_qkv_conv"][0].reshape(DEC_BATCH, QH, QT, P).transpose(3, 2, 0, 1)
                                      .reshape(P, QT, DEC_BATCH * QH)),
        "chist": np.ascontiguousarray(a["state_conv"][0].reshape(DEC_BATCH, CH, CT, P).transpose(3, 2, 0, 1)),
        "sdelta": np.ascontiguousarray(a["state_delta"][0].transpose(2, 1, 0, 3)),
        "memT": _rows(mem),
        "kT": np.ascontiguousarray(a["cache_mem_k"][0].reshape(DEC_BATCH, N_MEM, KB, P).transpose(0, 3, 2, 1)
                                   .reshape(DEC_BATCH, P, KB * N_MEM)),
        "v": np.ascontiguousarray(a["cache_mem_v"][0].reshape(DEC_BATCH, 2, P, D_MODEL).transpose(0, 2, 1, 3)
                                  .reshape(DEC_BATCH, P, 2 * D_MODEL)),
    }
    outputs = {
        "qlast": (P, QT, (1 + DEC_BATCH) * QH), "pconv": (P, CT, CH), "sconv": (P, CT, DEC_BATCH, CH),
        "sdelta_out": (P, HEADS, DEC_BATCH, DK), "pdelta_out": (P, HEADS, DK),
        "mk": (P, KB, N_MEM), "mv": (P, 2, D_MODEL), "yT": (P, KB, TOK),
    }
    nc = _bacc.Bacc("TRN2", target_bir_lowering=False, num_devices=1)
    f32 = mybir.dt.float32
    aps = {n: nc.dram_tensor(n, v.shape, f32, kind="ExternalInput").ap() for n, v in arrays.items()}
    aps.update({n: nc.dram_tensor(n, s, f32, kind="ExternalOutput").ap() for n, s in outputs.items()})
    build(nc, aps)
    r = _run(nc, [arrays], core_ids=[0]).results[0]

    y = r["yT"].transpose(2, 1, 0).reshape(TOK, D_MODEL)
    ql = r["qlast"].reshape(P, QT, 1 + DEC_BATCH, QH).transpose(2, 3, 1, 0).reshape(1 + DEC_BATCH, QH, 3 * HEADS * DK)
    return (y[None, :SEQ], y[SEQ:].reshape(DEC_BATCH, DEC_SEQ, D_MODEL),
            r["pconv"].transpose(2, 1, 0).reshape(1, 1, CH, CONV_CH), ql[None, :1],
            r["pdelta_out"].transpose(1, 0, 2)[None, None],
            r["mk"].transpose(2, 1, 0).reshape(1, 1, N_MEM, X_HEADS, X_DIM),
            r["mv"].transpose(1, 0, 2).reshape(1, 1, N_MEM, X_HEADS, X_DIM),
            r["sconv"].transpose(2, 3, 1, 0).reshape(1, DEC_BATCH, CH, CONV_CH), ql[None, 1:],
            r["sdelta_out"].transpose(2, 1, 0, 3)[None])
```
